# Optimizing a Trainium2 kernel written in Bass

```python
import jax, jax.numpy as jnp
from jax import lax
import numpy as np

'''One inference step of a hybrid autoregressive decoder trunk (DEPTH layers) for a prompt group and a sample group sharing the same weights.

Layer: x += W_o( sig(g_a) * A(h) + sig(g_b) * B(h) ),  h = RMSNorm(x);  x += MoE(RMSNorm(x)).
  A: causal multi-scale pooling mixer (4 channel groups, trailing windows 2/4/8/16, cumulative-sum means minus the token,
     per-group linear map, per-channel scale, projection to D_MODEL).
  B: short gated convolution mixer  W_out( Bg * conv3( Cg * v ) ), depthwise causal width-3 convolution.
  All of u_pool, Cg, Bg, v and both merge-gate logits come from ONE combined input projection w_in.
  MoE: softmax-over-top-4 router with bias, 32 experts, clamped SwiGLU (gpt-oss style).
16 learned meta tokens are prepended to each prompt sequence (positions 0..15) and dropped from y_prompt.

Inputs:
  x_prompt   (BATCH, SEQ, D_MODEL)
  x_sample   (DEC_BATCH, DEC_SEQ, D_MODEL)           positions PAST_LEN..PAST_LEN+DEC_SEQ-1
  state_pool (DEPTH, DEC_BATCH, POOL_BUF, D_POOL)    last 15 pooling-mixer input rows
  state_conv (DEPTH, DEC_BATCH, CONV_BUF, D_CONV)    last 2 convolution input rows (Cg * v)
  followed by the weights.
Returns (y_prompt, y_sample, new_pool_prompt, new_conv_prompt, new_pool_sample, new_conv_sample):
  y_prompt        (BATCH, SEQ, D_MODEL)
  y_sample        (DEC_BATCH, DEC_SEQ, D_MODEL)
  new_pool_prompt (DEPTH, BATCH, POOL_BUF, D_POOL)
  new_conv_prompt (DEPTH, BATCH, CONV_BUF, D_CONV)
  new_pool_sample (DEPTH, DEC_BATCH, POOL_BUF, D_POOL)
  new_conv_sample (DEPTH, DEC_BATCH, CONV_BUF, D_CONV)
'''

D_MODEL = 1024
BATCH = 1
SEQ = 256
DEPTH = 1
DEC_BATCH = 8
DEC_SEQ = 1
PAST_LEN = 2048
PAGE_SIZE = 128

N_META = 16
D_POOL = D_MODEL // 2
N_POOL_GROUPS = 4
POOL_GROUP = D_POOL // N_POOL_GROUPS
POOL_WINDOWS = (2, 4, 8, 16)
POOL_BUF = max(POOL_WINDOWS) - 1
D_CONV = D_MODEL // 2
CONV_WIDTH = 3
CONV_BUF = CONV_WIDTH - 1
D_IN_PROJ = D_POOL + 3 * D_CONV + 2 * D_MODEL
N_EXPERTS = 32
TOP_K = 4
D_FF = D_MODEL
SWIGLU_LIMIT = 7.0
SWIGLU_ALPHA = 1.702
MOE_BLOCK = 128
RMS_EPS = 1e-5

kernel_name = 'hybrid_pool_shortconv_moe_step'

def rms_norm(x, g):
    xf = x.astype(jnp.float32)
    y = xf * lax.rsqrt(jnp.mean(xf * xf, axis=-1, keepdims=True) + RMS_EPS)
    return (y * g.astype(jnp.float32)).astype(x.dtype)

def multiscale_pool(u, buf, p0):
    L = u.shape[1]
    ext = jnp.concatenate([buf, u], axis=1).astype(jnp.float32)
    cs = jnp.cumsum(ext, axis=1)
    cs = jnp.concatenate([jnp.zeros_like(cs[:, :1]), cs], axis=1)
    pos = p0 + jnp.arange(L)
    outs = []
    for g, w in enumerate(POOL_WINDOWS):
        sl = slice(g * POOL_GROUP, (g + 1) * POOL_GROUP)
        s = cs[:, POOL_BUF + 1:POOL_BUF + 1 + L, sl] - cs[:, POOL_BUF + 1 - w:POOL_BUF + 1 - w + L, sl]
        cnt = jnp.minimum(w, pos + 1).astype(jnp.float32)
        outs.append(s / cnt[None, :, None])
    mean = jnp.concatenate(outs, axis=-1)
    return (mean - u.astype(jnp.float32)).astype(u.dtype)

def short_conv(v, buf, w_conv):
    L = v.shape[1]
    ext = jnp.concatenate([buf, v], axis=1)
    return sum(ext[:, k:k + L] * w_conv[k] for k in range(CONV_WIDTH))

def moe_ffn(x, w_router, b_router, w_gu, b_gu, w_down, b_down):
    b, L, D = x.shape
    T = b * L
    xt = x.reshape(T, D)
    logits = (xt @ w_router).astype(jnp.float32) + b_router.astype(jnp.float32)
    top_val, top_idx = lax.top_k(logits, TOP_K)
    gates = jax.nn.softmax(top_val, axis=-1).astype(x.dtype)
    A = T * TOP_K
    e_flat = top_idx.reshape(A).astype(jnp.int32)
    g_flat = gates.reshape(A)
    tok_flat = jnp.arange(A, dtype=jnp.int32) // TOP_K
    order = jnp.argsort(e_flat)
    e_sorted = e_flat[order]
    counts = jnp.zeros((N_EXPERTS,), jnp.int32).at[e_flat].add(1)
    padded = (counts + MOE_BLOCK - 1) // MOE_BLOCK * MOE_BLOCK
    start = jnp.cumsum(counts) - counts
    pend = jnp.cumsum(padded)
    pstart = pend - padded
    rank = jnp.arange(A, dtype=jnp.int32) - start[e_sorted]
    dest = pstart[e_sorted] + rank
    n_blocks = -(-A // MOE_BLOCK) + N_EXPERTS
    R = n_blocks * MOE_BLOCK
    row_tok = jnp.full((R,), T, jnp.int32).at[dest].set(tok_flat[order])
    row_gate = jnp.zeros((R,), x.dtype).at[dest].set(g_flat[order])
    block_start = jnp.arange(n_blocks, dtype=jnp.int32) * MOE_BLOCK
    block_exp = jnp.minimum(jnp.searchsorted(pend, block_start, side='right'), N_EXPERTS - 1).astype(jnp.int32)
    x_pad = jnp.concatenate([xt, jnp.zeros((1, D), xt.dtype)], axis=0)
    xb = x_pad[row_tok].reshape(n_blocks, MOE_BLOCK, D)

    def expert_block(args):
        xblk, e = args
        hgu = xblk @ w_gu[e] + b_gu[e]
        gate = jnp.minimum(hgu[:, :D_FF], SWIGLU_LIMIT)
        up = jnp.clip(hgu[:, D_FF:], -SWIGLU_LIMIT, SWIGLU_LIMIT)
        act = gate * jax.nn.sigmoid(SWIGLU_ALPHA * gate) * (up + 1)
        return act @ w_down[e] + b_down[e]

    yb = lax.map(expert_block, (xb, block_exp))
    y = jax.ops.segment_sum(yb.reshape(R, D) * row_gate[:, None], row_tok, num_segments=T + 1)[:T]
    return y.reshape(b, L, D).astype(x.dtype)

def hybrid_layer(x, buf_pool, buf_conv, p0, g_mix, w_in, w_pool_grp, pool_scale, w_pool_up, w_conv,
                 w_conv_out, w_o, g_ffn, w_router, b_router, w_gu, b_gu, w_down, b_down):
    b, L, _ = x.shape
    h = rms_norm(x, g_mix)
    z = h @ w_in
    o1 = D_POOL
    o2 = o1 + D_CONV
    o3 = o2 + D_CONV
    o4 = o3 + D_CONV
    u_pool, c_gate, b_gate, v, gate_logits = z[..., :o1], z[..., o1:o2], z[..., o2:o3], z[..., o3:o4], z[..., o4:]
    pm = multiscale_pool(u_pool, buf_pool, p0)
    pm = jnp.einsum('blgc,gcd->blgd', pm.reshape(b, L, N_POOL_GROUPS, POOL_GROUP), w_pool_grp)
    branch_a = (pm.reshape(b, L, D_POOL) * pool_scale) @ w_pool_up
    cv = c_gate * v
    branch_b = (b_gate * short_conv(cv, buf_conv, w_conv)) @ w_conv_out
    gates = jax.nn.sigmoid(gate_logits.astype(jnp.float32)).astype(x.dtype)
    g_a, g_b = gates[..., :D_MODEL], gates[..., D_MODEL:]
    x = x + (g_a * branch_a + g_b * branch_b) @ w_o
    x = x + moe_ffn(rms_norm(x, g_ffn), w_router, b_router, w_gu, b_gu, w_down, b_down)
    new_pool = jnp.concatenate([buf_pool, u_pool], axis=1)[:, -POOL_BUF:]
    new_conv = jnp.concatenate([buf_conv, cv], axis=1)[:, -CONV_BUF:]
    return x, new_pool, new_conv

def setup_inputs(seed: int = 0) -> dict:
    key = jax.random.key(seed)
    ks = jax.random.split(key, 24)
    n = jax.random.normal
    f32 = jnp.float32
    return {
        'x_prompt': n(ks[0], (BATCH, SEQ, D_MODEL), f32),
        'x_sample': n(ks[1], (DEC_BATCH, DEC_SEQ, D_MODEL), f32),
        'state_pool': n(ks[2], (DEPTH, DEC_BATCH, POOL_BUF, D_POOL), f32),
        'state_conv': n(ks[3], (DEPTH, DEC_BATCH, CONV_BUF, D_CONV), f32),
        'meta_tokens': n(ks[4], (N_META, D_MODEL), f32),
        'g_mix': 1.0 + 0.01 * n(ks[5], (DEPTH, D_MODEL), f32),
        'w_in': n(ks[6], (DEPTH, D_MODEL, D_IN_PROJ), f32) * D_MODEL ** -0.5,
        'w_pool_grp': n(ks[7], (DEPTH, N_POOL_GROUPS, POOL_GROUP, POOL_GROUP), f32) * POOL_GROUP ** -0.5,
        'pool_scale': 1.0 + 0.02 * n(ks[8], (DEPTH, D_POOL), f32),
        'w_pool_up': n(ks[9], (DEPTH, D_POOL, D_MODEL), f32) * D_POOL ** -0.5,
        'w_conv': n(ks[10], (DEPTH, CONV_WIDTH, D_CONV), f32) * CONV_WIDTH ** -0.5,
        'w_conv_out': n(ks[11], (DEPTH, D_CONV, D_MODEL), f32) * D_CONV ** -0.5,
        'w_o': n(ks[12], (DEPTH, D_MODEL, D_MODEL), f32) * D_MODEL ** -0.5,
        'g_ffn': 1.0 + 0.01 * n(ks[13], (DEPTH, D_MODEL), f32),
        'w_router': n(ks[14], (DEPTH, D_MODEL, N_EXPERTS), f32) * D_MODEL ** -0.5,
        'b_router': 0.01 * n(ks[15], (DEPTH, N_EXPERTS), f32),
        'w_gu': n(ks[16], (DEPTH, N_EXPERTS, D_MODEL, 2 * D_FF), f32) * D_MODEL ** -0.5,
        'b_gu': 0.01 * n(ks[17], (DEPTH, N_EXPERTS, 2 * D_FF), f32),
        'w_down': n(ks[18], (DEPTH, N_EXPERTS, D_FF, D_MODEL), f32) * D_FF ** -0.5,
        'b_down': 0.01 * n(ks[19], (DEPTH, N_EXPERTS, D_MODEL), f32),
        'g_final': 1.0 + 0.01 * n(ks[20], (D_MODEL,), f32),
    }

def reference(x_prompt, x_sample, state_pool, state_conv, meta_tokens, g_mix, w_in, w_pool_grp, pool_scale,
              w_pool_up, w_conv, w_conv_out, w_o, g_ffn, w_router, b_router, w_gu, b_gu, w_down, b_down, g_final):
    bp = x_prompt.shape[0]
    meta = jnp.broadcast_to(meta_tokens[None].astype(x_prompt.dtype), (bp, N_META, D_MODEL))
    hp = jnp.concatenate([meta, x_prompt], axis=1)
    hs = x_sample
    zero_pool = jnp.zeros((bp, POOL_BUF, D_POOL), hp.dtype)
    zero_conv = jnp.zeros((bp, CONV_BUF, D_CONV), hp.dtype)
    pool_p, conv_p, pool_s, conv_s = [], [], [], []
    for l in range(DEPTH):
        wl = (g_mix[l], w_in[l], w_pool_grp[l], pool_scale[l], w_pool_up[l], w_conv[l], w_conv_out[l], w_o[l],
              g_ffn[l], w_router[l], b_router[l], w_gu[l], b_gu[l], w_down[l], b_down[l])
        hp, npool, nconv = hybrid_layer(hp, zero_pool, zero_conv, 0, *wl)
        pool_p.append(npool)
        conv_p.append(nconv)
        hs, spool, sconv = hybrid_layer(hs, state_pool[l], state_conv[l], PAST_LEN, *wl)
        pool_s.append(spool)
        conv_s.append(sconv)
    y_prompt = rms_norm(hp[:, N_META:], g_final)
    y_sample = rms_norm(hs, g_final)
    return (y_prompt, y_sample, jnp.stack(pool_p), jnp.stack(conv_p), jnp.stack(pool_s), jnp.stack(conv_s))


_drawn_inputs = setup_inputs


def setup_inputs(seed=0):
    import zlib

    import numpy as np

    out = dict(_drawn_inputs(seed))
    spreads = {}
    factors = {'b_gu': 8.0, 'b_down': 8.0, 'g_final': 5.868}
    for name, (base, spread) in spreads.items():
        noise = np.random.default_rng([zlib.crc32(name.encode()), seed]).standard_normal(out[name].shape)
        drawn = base * np.exp(spread * noise) if base else spread * noise
        out[name] = __import__('jax').numpy.asarray(drawn.astype(out[name].dtype))
    for name, factor in factors.items():
        out[name] = (out[name] * factor).astype(out[name].dtype)
    return out
```

```python
from contextlib import ExitStack

import concourse.bass as bass
from concourse import mybir

ALU = mybir.AluOpType
ACT = mybir.ActivationFunctionType
AXX = mybir.AxisListType.X
F32 = mybir.dt.float32
I32 = mybir.dt.int32
U32 = mybir.dt.uint32

P = 128
D = 1024
KT = D // P
HALF = 512
CH = HALF // P
META, PROMPT, SAMPLE = 16, 256, 8
TOK = PROMPT + SAMPLE
COLS = META + TOK
NT = 3
WINDOWS = (2, 4, 8, 16)
PBUF, CBUF, CW = 15, 2, 3
E, TOPK = 32, 4
SLOTS = 64
ROUNDS = -(-TOK // SLOTS)
ITEMS = ROUNDS * E
LIMIT, ALPHA, EPS = 7.0, 1.702, 1e-5
NCHUNK = 32


def build(nc, x_prompt, x_sample, state_pool, state_conv, meta_tokens, g_mix, w_in, w_pool_grp, pool_scale,
          w_pool_up, w_conv, w_conv_out, w_o, g_ffn, w_router, b_router, w_gu, b_gu, w_down, b_down, g_final,
          y_prompt, y_sample, new_pool_prompt, new_conv_prompt, new_pool_sample, new_conv_sample):
    with ExitStack() as ctx:
        def sb(name, shape, dt=F32):
            return ctx.enter_context(nc.sbuf_tensor(name, shape, dt))

        def sem(name):
            return ctx.enter_context(nc.semaphore(name))

        gu_ring = sb("gu_ring", [P, 2 * KT, 2 * D])
        down_ring = sb("down_ring", [P, KT, D])
        Y = sb("Y", [P, NT, D])
        XN = sb("XN", [P, NT, D])
        work = sb("work", [P, 2112])
        table = sb("table", [P, ITEMS + 2, 2 * NT])
        bias_gu = sb("bias_gu", [P, E, 2, CH, 2])
        ident = sb("ident", [P, P])
        slot_no = sb("slot_no", [P, SLOTS])
        pick = sb("pick", [P, NT, SLOTS])
        pick_gate = sb("pick_gate", [P, NT, 2 * SLOTS])
        XgT = sb("XgT", [P, KT, SLOTS])
        spread = sb("spread", [P, NT, P])
        actT = sb("actT", [P, CH, 2, SLOTS])
        yb = sb("yb", [P, HALF])
        params = sb("params", [P, 24])
        cur = sb("cur", [P, 2 * NT])
        stat = sb("stat", [P, 4, NT])
        rounds_sb = sb("rounds_sb", [P, 1], I32)
        PS = ctx.enter_context(nc.psum_tensor("PS", [P, 8, HALF], F32))

        hgu = work[:, 0:1024]
        sig = work[:, 1024:1536]
        poolT = work[:, 0:480].rearrange("p (c b r) -> p c b r", c=CH, r=PBUF)
        convT = work[:, 480:544].rearrange("p (c b r) -> p c b r", c=CH, r=CBUF)
        tail_u = work[:, 544:1056]
        tail_cv = work[:, 1056:1568]
        scr_a = work[:, 1568:1840]
        scr_b = work[:, 1840:2112]
        xn2T = work[:, 0:KT * TOK].rearrange("p (k t) -> p k t", t=TOK)

        low = gu_ring[:, KT:2 * KT, :].rearrange("p k n -> p (k n)")
        hT = low[:, 0:2240].rearrange("p (k t) -> p k t", t=COLS)
        uT = low[:, 2240:3360].rearrange("p (k t) -> p k t", t=COLS)
        cT = low[:, 3360:4480].rearrange("p (k t) -> p k t", t=COLS)
        bT = low[:, 4480:5536].rearrange("p (k t) -> p k t", t=TOK)
        cvT = low[:, 5536:6656].rearrange("p (k t) -> p k t", t=COLS)
        gatesT = low[:, 6656:10880].rearrange("p (k t) -> p k t", t=TOK)
        pmT = low[:, 10880:11936].rearrange("p (k t) -> p k t", t=TOK)
        paT = low[:, 11936:12992].rearrange("p (k t) -> p k t", t=TOK)
        cbT = low[:, 12992:14048].rearrange("p (k t) -> p k t", t=TOK)
        mT = low[:, 14048:16160].rearrange("p (k t) -> p k t", t=TOK)
        below = low[:, 16160:16288]
        bgu_rows = low[0:E, 6656:8704]
        pool_rows = low[0:SAMPLE * PBUF, 8704:9216]
        conv_rows = low[0:SAMPLE * CBUF, 9216:9728]
        param_rows = low[0:24, 9728:9856]
        grp = low[:, 14048:14560].rearrange("p (g d) -> p g d", g=CH)
        spare = sb("spare", [P, 1])
        g_ffn_all = low[:, 0:1024]
        bdown_rows = low[0:E, 1024:2048]
        wr = low[:, 3360:3616].rearrange("p (k e) -> p k e", e=E)
        br_all = low[:, 3616:3648]
        samp_stage = low[0:SAMPLE, 10880:11904]
        rt = 4480

        def route(n):
            nonlocal rt
            rt += n
            assert rt <= 6656
            return low[:, rt - n:rt]

        ones = route(P)
        logits = route(NT * E).rearrange("p (t e) -> p t e", e=E)
        top = route(NT * 8).rearrange("p (t e) -> p t e", e=8)
        topi = route(NT * 8).rearrange("p (t e) -> p t e", e=8)
        topf = route(NT * 8).rearrange("p (t e) -> p t e", e=8)
        ex = route(NT * TOPK).rearrange("p (t e) -> p t e", e=TOPK)
        exs = route(NT)
        valid = route(NT)
        hot = route(NT * TOPK * E).rearrange("p (t k e) -> p t k e", k=TOPK, e=E)
        hotg = route(NT * TOPK * E).rearrange("p (t k e) -> p t k e", k=TOPK, e=E)
        mask = route(NT * E).rearrange("p (t e) -> p t e", e=E)
        G = route(NT * E).rearrange("p (t e) -> p t e", e=E)
        pos1 = route(NT * E).rearrange("p (t e) -> p t e", e=E)
        GT = route(TOK)
        most = route(1)
        over = route(ROUNDS - 1)
        bounds = route(ROUNDS - 1)

        pool_up = gu_ring[:, 0:2, :].rearrange("p s n -> p (s n)").rearrange("p (k n) -> p k n", k=CH)
        conv_out = gu_ring[:, 2:4, :].rearrange("p s n -> p (s n)").rearrange("p (k n) -> p k n", k=CH)

        win_landed = [sem(f"win_landed{s}") for s in range(KT)]
        x_landed = sem("x_landed")
        rows_landed = sem("rows_landed")
        grp_landed = sem("grp_landed")
        up_landed = sem("up_landed")
        convout_landed = sem("convout_landed")
        wo_landed = sem("wo_landed")
        late_landed = sem("late_landed")
        consts = sem("consts")
        rows_turned = sem("rows_turned")
        rows_kept = sem("rows_kept")
        squared = sem("squared")
        rooted = sem("rooted")
        normed = sem("normed")
        x_turned = sem("x_turned")
        h_ready = sem("h_ready")
        z_done = sem("z_done")
        z_kept = sem("z_kept")
        cv_done = sem("cv_done")
        dve = sem("dve")
        cb_ready = sem("cb_ready")
        pm_ready = sem("pm_ready")
        tails_turned = sem("tails_turned")
        tails_kept = sem("tails_kept")
        grp_done = sem("grp_done")
        pa_ready = sem("pa_ready")
        branches = sem("branches")
        mixed = sem("mixed")
        wo_done = sem("wo_done")
        samp_staged = sem("samp_staged")
        resid = sem("resid")
        x2_turned = sem("x2_turned")
        x2_kept = sem("x2_kept")
        logits_done = sem("logits_done")
        shifted = sem("shifted")
        exped = sem("exped")
        mask_ready = sem("mask_ready")
        ranks = sem("ranks")
        gt_turned = sem("gt_turned")
        gt_kept = sem("gt_kept")
        bd_done = sem("bd_done")
        rounds_ready = sem("rounds_ready")
        stored = sem("stored")
        gu_landed = [sem(f"gu_landed{s}") for s in range(2 * KT)]
        down_landed = [sem(f"down_landed{q}") for q in range(CH)]
        gu_used = sem("gu_used")
        down_used = sem("down_used")
        pick_ready = sem("pick_ready")
        pick_gate_ready = sem("pick_gate_ready")
        gathered = sem("gathered")
        xg_ready = sem("xg_ready")
        spread_turned = sem("spread_turned")
        spread_ready = sem("spread_ready")
        gate_kept = sem("gate_kept")
        up_kept = sem("up_kept")
        gate_turned = sem("gate_turned")
        up_turned = sem("up_turned")
        cur_ready = sem("cur_ready")
        g_biased = sem("g_biased")
        g_ready = sem("g_ready")
        u_biased = sem("u_biased")
        u_ready = sem("u_ready")
        sig_ready = sem("sig_ready")
        gu_product = sem("gu_product")
        act_ready = sem("act_ready")
        yb_ready = sem("yb_ready")
        scattered = sem("scattered")
        added = sem("added")
        gfin_landed = sem("gfin_landed")
        fin = sem("fin")

        block = ctx.enter_context(nc.Block())

        def z_evacuated(pe, n):
            if n < 12:
                pe.wait_ge(z_kept, n + 1)
            elif n < 16:
                pe.wait_ge(cv_done, n - 11)
            else:
                pe.wait_ge(z_kept, n - 3)

        @block.sync
        def _(sp):
            for n in range(16):
                if n == 8:
                    sp.dma_start(down_ring[:], w_o[0].rearrange("(k p) n -> p k n", p=P)).then_inc(wo_landed, 16)
                if n >= 8:
                    sp.wait_ge(z_done, 2 * (n - 8) + 2)
                sp.dma_start(gu_ring[:, n % 8, :].rearrange("p (k n) -> p k n", k=KT),
                             w_in[0, :, 256 * n:256 * n + 256].rearrange("(k p) n -> p k n", p=P)
                             ).then_inc(win_landed[n % 8], 16)
            sp.wait_ge(z_done, 20)
            sp.dma_start(pool_up, w_pool_up[0].rearrange("(k p) n -> p k n", p=P)).then_inc(up_landed, 16)
            sp.wait_ge(z_done, 24)
            sp.dma_start(conv_out, w_conv_out[0].rearrange("(k p) n -> p k n", p=P)).then_inc(convout_landed, 16)

            def load_gu(e, parity, k, dynamic):
                src = w_gu[0, bass.ds(e, 1), k * P:(k + 1) * P, :].rearrange("a p n -> (a p) n") if dynamic \
                    else w_gu[0, e, k * P:(k + 1) * P, :]
                sp.dma_start(gu_ring[:, KT * parity + k, :], src).then_inc(gu_landed[KT * parity + k], 16)

            def load_down(e, q, dynamic):
                src = w_down[0, bass.ds(e, 1), 2 * q * P:(2 * q + 2) * P, :].rearrange("a (k p) n -> p (a k) n", p=P) \
                    if dynamic else w_down[0, e, 2 * q * P:(2 * q + 2) * P, :].rearrange("(k p) n -> p k n", p=P)
                sp.dma_start(down_ring[:, 2 * q:2 * q + 2, :], src).then_inc(down_landed[q], 16)

            for k in (4, 5, 6, 7, 0, 1, 2, 3):
                if k >= 4:
                    sp.wait_ge(z_done, 2 * (8 + k) + 2)
                else:
                    sp.wait_ge(branches, 8)
                load_gu(0, 0, k, False)
            sp.wait_ge(wo_done, 5)
            for q in range(CH):
                load_down(0, q, False)
            sp.wait_ge(bd_done, NT)
            sp.wait_ge(rounds_ready, 2)
            for k in range(KT):
                load_gu(1, 1, k, False)

            def item_down(i, e):
                for q in range(CH):
                    sp.wait_ge(down_used, 4 * i + (q - 3))
                    load_down(e, q, True)

            def item_gu(i, e, parity):
                for k in range(KT):
                    sp.wait_ge(gu_used, 8 * i + (k - 15))
                    load_gu(e, parity, k, True)

            with sp.Fori(0, E // 2 - 1) as pair:
                i = sp.snap(2 * pair + 1)
                e1 = sp.snap(2 * pair + 2)
                e2 = sp.snap(2 * pair + 3)
                item_down(i, i)
                item_gu(i + 1, e1, 0)
                item_down(i + 1, e1)
                item_gu(i + 2, e2, 1)
            for q in range(CH):
                sp.wait_ge(down_used, 4 * (E - 1) + q - 3)
                load_down(E - 1, q, False)

            rounds = sp.value_load(rounds_sb[0:1, 0:1], min_val=1, max_val=ROUNDS)
            with sp.If(rounds > 1):
                with sp.Fori(1, rounds) as r:
                    with sp.Fori(0, E // 2) as pair:
                        for u in range(2):
                            eu = sp.snap(2 * pair + u)
                            i = sp.snap(r * E + eu)
                            item_gu(i, eu, u)
                            item_down(i, eu)
            sp.wait_ge(gathered, rounds * E + 1)
            sp.dma_start(XN[:, 0, :], g_final.rearrange("(a n) -> a n", a=1).to_broadcast([P, D])
                         ).then_inc(gfin_landed, 16)
            for t in range(2):
                sp.wait_ge(fin, t + 1)
                sp.dma_start(y_prompt[0, t * P:(t + 1) * P, :], Y[:, t, :]).then_inc(stored, 16)
            sp.wait_ge(fin, 3)
            sp.dma_start(y_sample[:, 0, :], Y[0:SAMPLE, 2, :]).then_inc(stored, 16)
            sp.wait_ge(stored, 16 * 9)

        @block.gpsimd
        def _(pool):
            nc.gpsimd.memset(ident[:], 0.0).then_inc(consts, 1)
            nc.gpsimd.memset(below, 1.0).then_inc(consts, 1)
            nc.gpsimd.memset(table[:], -1.0).then_inc(consts, 1)
            nc.gpsimd.iota(scr_a.bitcast(I32)[:, 0:SLOTS], pattern=[[1, SLOTS]], base=0,
                           channel_multiplier=0).then_inc(consts, 1)
            pool.wait_ge(consts, 4)
            nc.gpsimd.affine_select(out=ident[:], in_=ident[:], compare_op=ALU.not_equal, fill=1.0, base=0,
                                    pattern=[[-1, P]], channel_multiplier=1).then_inc(consts, 1)
            nc.gpsimd.affine_select(out=below, in_=below, compare_op=ALU.is_gt, fill=0.0, base=0,
                                    pattern=[[1, P]], channel_multiplier=-1).then_inc(consts, 1)
            nc.gpsimd.tensor_copy(slot_no[:], scr_a.bitcast(I32)[:, 0:SLOTS]).then_inc(consts, 1)

        @block.scalar
        def _(act):
            act.dma_start(Y[:, 0, :], x_prompt[0, 0:P, :]).then_inc(x_landed, 16)
            act.dma_start(Y[:, 1, :], x_prompt[0, P:2 * P, :]).then_inc(x_landed, 16)
            act.dma_start(Y[0:SAMPLE, 2, :], x_sample[:, 0, :]).then_inc(x_landed, 16)
            act.dma_start(Y[SAMPLE:SAMPLE + META, 2, :], meta_tokens).then_inc(x_landed, 16)
            act.dma_start(param_rows[0:8, :], g_mix[0].rearrange("(k p) -> k p", p=P)).then_inc(rows_landed, 16)
            act.dma_start(param_rows[8:12, :], pool_scale[0].rearrange("(k p) -> k p", p=P)).then_inc(rows_landed, 16)
            act.dma_start(param_rows[12:24, :], w_conv[0].rearrange("w (k p) -> (w k) p", p=P)
                          ).then_inc(rows_landed, 16)
            act.dma_start(grp, w_pool_grp[0].rearrange("g c d -> c g d")).then_inc(grp_landed, 16)
            act.dma_start(bgu_rows, b_gu[0]).then_inc(rows_landed, 16)
            act.dma_start(pool_rows, state_pool[0].rearrange("b r d -> (b r) d")).then_inc(rows_landed, 16)
            act.dma_start(conv_rows, state_conv[0].rearrange("b r d -> (b r) d")).then_inc(rows_landed, 16)
            act.dma_start(new_pool_sample[0, :, 0:PBUF - 1, :], state_pool[0, :, 1:PBUF, :]).then_inc(stored, 16)
            act.dma_start(new_conv_sample[0, :, 0:CBUF - 1, :], state_conv[0, :, 1:CBUF, :]).then_inc(stored, 16)

            def sum_squares(t, rows, squares):
                nc.scalar.activation(squares, Y[rows, t, :], ACT.Square,
                                     accum_out=stat[rows, 0, t:t + 1]).then_inc(squared, 1)

            act.wait_ge(x_landed, 64)
            act.wait_ge(dve, 2)
            for t in range(NT):
                rows = slice(0, P if t < 2 else SAMPLE + META)
                sum_squares(t, rows, XN[rows, t, :])
            act.wait_ge(normed, 1)
            nc.scalar.activation(stat[:, 2, :], stat[:, 1, :], ACT.Sqrt).then_inc(rooted, 1)

            for n in range(12):
                dst, cols = ((uT, COLS), (cT, COLS), (bT, TOK))[n // 4]
                act.wait_ge(z_done, n + 1)
                nc.scalar.activation(dst[:, n % 4, :], PS[:, n % 4, 0:cols], ACT.Copy).then_inc(z_kept, 1)
            for n in range(16, 32):
                act.wait_ge(z_done, n + 1)
                nc.scalar.activation(gatesT[:, n - 16, :], PS[:, n % 4, 0:TOK], ACT.Sigmoid).then_inc(z_kept, 1)
                if n == 19:
                    act.wait_ge(tails_turned, 2)
                    nc.scalar.activation(tail_u[0:PBUF + SAMPLE, :], PS[0:PBUF + SAMPLE, 5, :],
                                         ACT.Copy).then_inc(tails_kept, 1)
                    nc.scalar.activation(tail_cv[0:CBUF + SAMPLE, :], PS[0:CBUF + SAMPLE, 6, :],
                                         ACT.Copy).then_inc(tails_kept, 1)
                    act.wait_ge(tails_kept, 2)
                    act.dma_start(new_pool_prompt[0, 0], tail_u[0:PBUF, :]).then_inc(stored, 16)
                    act.dma_start(new_pool_sample[0, :, PBUF - 1, :], tail_u[PBUF:PBUF + SAMPLE, :]
                                  ).then_inc(stored, 16)
                    act.dma_start(new_conv_prompt[0, 0], tail_cv[0:CBUF, :]).then_inc(stored, 16)
                    act.dma_start(new_conv_sample[0, :, CBUF - 1, :], tail_cv[CBUF:CBUF + SAMPLE, :]
                                  ).then_inc(stored, 16)
            act.wait_ge(z_done, 32)
            act.dma_start(g_ffn_all, g_ffn.to_broadcast([P, D])).then_inc(late_landed, 16)
            act.dma_start(bdown_rows, b_down[0]).then_inc(late_landed, 16)
            act.wait_ge(cv_done, 4)
            act.dma_start(wr, w_router[0].rearrange("(k p) e -> p k e", p=P)).then_inc(late_landed, 16)
            act.dma_start(br_all, b_router.to_broadcast([P, E])).then_inc(late_landed, 16)

            act.wait_ge(wo_done, 5)
            for q in range(4):
                nc.scalar.activation(samp_stage[:, 256 * q:256 * q + 256], PS[32 * q:32 * q + SAMPLE, 4, 0:256],
                                     ACT.Copy).then_inc(samp_staged, 1)
            for t in range(NT):
                act.wait_ge(resid, t + 1)
                rows = slice(0, P if t < 2 else SAMPLE)
                sum_squares(t, rows, XN[rows, t, :])
            act.wait_ge(normed, 5)
            nc.scalar.activation(stat[:, 2, :], stat[:, 1, :], ACT.Sqrt).then_inc(rooted, 1)
            act.wait_ge(stored, 16 * 6)
            for t in range(NT):
                act.wait_ge(x2_turned, t + 1)
                if t < 2:
                    for q in range(2):
                        bank = (5 + 2 * t + q) % 8
                        nc.scalar.activation(xn2T[:, 4 * q:4 * q + 4, P * t:P * t + P],
                                             PS[:, bank, :].rearrange("p (k t) -> p k t", k=4),
                                             ACT.Copy).then_inc(x2_kept, 1)
                else:
                    nc.scalar.activation(xn2T[:, :, 2 * P:TOK],
                                         PS[:, 1, 0:KT * SAMPLE].rearrange("p (k t) -> p k t", k=KT),
                                         ACT.Copy).then_inc(x2_kept, 1)
            act.wait_ge(shifted, 1)
            nc.scalar.activation(ex, ex, ACT.Exp).then_inc(exped, 1)
            act.wait_ge(gt_turned, 1)
            nc.scalar.activation(GT[0:E, :], PS[0:E, 4, 0:TOK], ACT.Copy).then_inc(gt_kept, 1)

            def keep_gathered(count):
                act.wait_ge(gathered, count)
                nc.scalar.activation(XgT[:].rearrange("p k s -> p (k s)"), PS[:, 5, :], ACT.Copy).then_inc(xg_ready, 1)

            keep_gathered(1)
            act.wait_ge(rounds_ready, 2)
            rounds = act.value_load(rounds_sb[0:1, 0:1], min_val=1, max_val=ROUNDS)
            with act.Fori(0, rounds * E) as i:
                act.wait_ge(gu_used, 8 * i + 8)
                nc.scalar.activation(hgu[:, 0:HALF], PS[:, 0, :], ACT.Copy).then_inc(gate_kept, 1)
                keep_gathered(i + 2)
                act.wait_ge(spread_turned, i + 1)
                nc.scalar.activation(spread[:].rearrange("p t s -> p (t s)"), PS[:, 4, 0:NT * P],
                                     ACT.Copy).then_inc(spread_ready, 1)
                act.wait_ge(g_ready, i + 1)
                nc.scalar.activation(sig, hgu[:, 0:HALF], ACT.Sigmoid, scale=ALPHA).then_inc(sig_ready, 1)
                act.wait_ge(down_used, 4 * i + 4)
                nc.scalar.activation(yb[:], PS[:, 4, :], ACT.Copy).then_inc(yb_ready, 1)
            for t in range(NT):
                act.wait_ge(added, rounds * (3 * E) + (t + 4))
                rows = slice(0, P if t < 2 else SAMPLE)
                sum_squares(t, rows, XN[rows, t, :] if t else work[:, 0:D])
            act.wait_ge(normed, 9)
            nc.scalar.activation(stat[:, 2, :], stat[:, 1, :], ACT.Sqrt).then_inc(rooted, 1)

        @block.tensor
        def _(pe):
            mm = nc.tensor.matmul
            pe.wait_ge(consts, 7)
            pe.wait_ge(rows_landed, 96)
            nc.tensor.transpose(PS[:, 4, 0:24], param_rows, ident[0:24, 0:24]).then_inc(rows_turned, 1)
            for c in range(16):
                last = nc.tensor.transpose(PS[:, 5, E * c:E * c + E], bgu_rows[:, P * c:P * c + P], ident[0:E, 0:E])
            last.then_inc(rows_turned, 1)
            n = SAMPLE * PBUF
            for c in range(CH):
                last = nc.tensor.transpose(PS[:, 6, n * c:n * c + n], pool_rows[:, P * c:P * c + P], ident[0:n, 0:n])
            last.then_inc(rows_turned, 1)
            n = SAMPLE * CBUF
            for c in range(CH):
                last = nc.tensor.transpose(PS[:, 7, n * c:n * c + n], conv_rows[:, P * c:P * c + P], ident[0:n, 0:n])
            last.then_inc(rows_turned, 1)

            pe.wait_ge(rows_kept, 1)
            for t in range(NT):
                pe.wait_ge(normed, 2 + t)
                rows = P if t < 2 else SAMPLE + META
                for k in range(KT):
                    out = PS[:, 2 * t + k // 4, P * (k % 4):P * (k % 4) + P] if t < 2 else PS[:, 4, rows * k:rows * k + rows]
                    last = nc.tensor.transpose(out, XN[0:rows, t, P * k:P * k + P], ident[0:rows, 0:rows])
                last.then_inc(x_turned, 1)

            pe.wait_ge(h_ready, 6)
            for n in range(NCHUNK):
                lo = 0 if n < 8 or 12 <= n < 16 else META
                b = n // 2
                if n % 2 == 0:
                    pe.wait_ge(win_landed[b % 8], 16 * (b // 8 + 1))
                if n >= 4:
                    z_evacuated(pe, n - 4)
                w = gu_ring[:, b % 8, :].rearrange("p (k n) -> p k n", k=KT)
                for k in range(KT):
                    last = mm(PS[:, n % 4, 0:COLS - lo], w[:, k, P * (n % 2):P * (n % 2) + P], hT[:, k, lo:COLS],
                              start=(k == 0), stop=(k == KT - 1))
                last.then_inc(z_done, 1)
                if n == 17:
                    pe.wait_ge(cv_done, 4)
                    pe.wait_ge(rows_kept, 5)
                    for c in range(CH):
                        last = nc.tensor.transpose(PS[0:PBUF + SAMPLE, 5, P * c:P * c + P],
                                                   uT[:, c, COLS - SAMPLE - PBUF:COLS], ident[:])
                    last.then_inc(tails_turned, 1)
                    for c in range(CH):
                        last = nc.tensor.transpose(PS[0:CBUF + SAMPLE, 6, P * c:P * c + P],
                                                   cvT[:, c, COLS - SAMPLE - CBUF:COLS], ident[:])
                    last.then_inc(tails_turned, 1)

            pe.wait_ge(tails_kept, 2)
            pe.wait_ge(pm_ready, 4)
            pe.wait_ge(grp_landed, 16)
            for g in range(CH):
                mm(PS[:, 4 + g, 0:TOK], grp[:, g, :], pmT[:, g, :], start=True, stop=True).then_inc(grp_done, 1)

            pe.wait_ge(pa_ready, 4)
            pe.wait_ge(cb_ready, 4)
            pe.wait_ge(up_landed, 16)
            pe.wait_ge(convout_landed, 16)
            for m in range(KT):
                if m >= 2:
                    pe.wait_ge(mixed, m - 1)
                for k in range(CH):
                    mm(PS[:, 4 + 2 * (m % 2), 0:TOK], pool_up[:, k, P * m:P * m + P], paT[:, k, :],
                       start=(k == 0), stop=(k == CH - 1))
                for k in range(CH):
                    last = mm(PS[:, 5 + 2 * (m % 2), 0:TOK], conv_out[:, k, P * m:P * m + P], cbT[:, k, :],
                              start=(k == 0), stop=(k == CH - 1))
                last.then_inc(branches, 1)

            pe.wait_ge(mixed, 8)
            pe.wait_ge(wo_landed, 16)
            pe.wait_ge(z_kept, 28)
            for t in range(2):
                for h in range(2):
                    for k in range(KT):
                        last = mm(PS[:, 2 * t + h, :], mT[:, k, P * t:P * t + P],
                                  down_ring[:, k, HALF * h:HALF * h + HALF], start=(k == 0), stop=(k == KT - 1))
                    last.then_inc(wo_done, 1)
            for k in range(KT):
                for q in range(4):
                    last = mm(PS[32 * q:32 * q + SAMPLE, 4, 0:256], mT[:, k, 2 * P:TOK],
                              down_ring[:, k, 256 * q:256 * q + 256], start=(k == 0), stop=(k == KT - 1))
            last.then_inc(wo_done, 1)

            pe.wait_ge(late_landed, 64)
            for t in range(NT):
                pe.wait_ge(normed, 6 + t)
                rows = P if t < 2 else SAMPLE
                for k in range(KT):
                    bank = (5 + 2 * t + k // 4) % 8
                    out = PS[:, bank, P * (k % 4):P * (k % 4) + P] if t < 2 else PS[:, 1, rows * k:rows * k + rows]
                    last = nc.tensor.transpose(out, XN[0:rows, t, P * k:P * k + P], ident[0:rows, 0:rows])
                last.then_inc(x2_turned, 1)
            for t in range(NT):
                pe.wait_ge(x2_kept, (2, 4, 5)[t])
                rows = P if t < 2 else SAMPLE
                for k in range(KT):
                    last = mm(PS[0:rows, 2, E * t:E * t + E], xn2T[:, k, P * t:P * t + rows], wr[:, k, :],
                              start=(k == 0), stop=(k == KT - 1))
                last.then_inc(logits_done, 1)

            pe.wait_ge(mask_ready, 1)
            for t in range(NT):
                for s in range(t + 1):
                    mm(PS[:, 3, E * t:E * t + E], below if s == t else ones, mask[:, s, :],
                       start=(s == 0), stop=(s == t))
            for s in range(NT):
                last = mm(PS[:, 3, E * NT:E * NT + E], ones, mask[:, s, :], start=(s == 0), stop=(s == NT - 1))
            last.then_inc(ranks, 1)
            pe.wait_ge(mask_ready, 2)
            for t in range(NT):
                rows = P if t < 2 else SAMPLE
                last = nc.tensor.transpose(PS[0:E, 4, P * t:P * t + rows], G[0:rows, t, :], ident[0:rows, 0:rows])
            last.then_inc(gt_turned, 1)

            def gather():
                for k in range(KT):
                    for t in range(NT):
                        last = mm(PS[:, 5, SLOTS * k:SLOTS * k + SLOTS], XN[:, t, P * k:P * k + P], pick[:, t, :],
                                  start=(t == 0), stop=(t == NT - 1))
                last.then_inc(gathered, 1)

            def scatter(t):
                for h in range(2):
                    last = mm(PS[:, 6 + h, :], spread[SLOTS * h:SLOTS * h + SLOTS, t, :],
                              yb[SLOTS * h:SLOTS * h + SLOTS, :], start=True, stop=True)
                last.then_inc(scattered, 1)

            pe.wait_ge(pick_ready, 1)
            gather()
            pe.wait_ge(gt_kept, 1)
            for t in range(NT):
                rows = P if t < 2 else SAMPLE
                if t:
                    pe.wait_ge(added, t)
                for h in range(2):
                    last = mm(PS[0:rows, 6 + h, :], GT[0:E, P * t:P * t + rows],
                              bdown_rows[:, HALF * h:HALF * h + HALF], start=True, stop=True)
                last.then_inc(bd_done, 1)
            pe.wait_ge(added, 3)
            pe.wait_ge(rounds_ready, 2)
            rounds = pe.value_load(rounds_sb[0:1, 0:1], min_val=1, max_val=ROUNDS)
            with pe.Fori(0, rounds * (E // 2)) as pair:
                for u in range(2):
                    i = 2 * pair + u
                    pe.wait_ge(xg_ready, i + 1)
                    for k in range(KT):
                        pe.wait_ge(gu_landed[KT * u + k], 16 * pair + 16)
                        w = gu_ring[:, KT * u + k, :]
                        for b in range(2):
                            for h in range(2):
                                last = mm(PS[SLOTS * h:SLOTS * h + SLOTS, b, :], XgT[:, k, :],
                                          w[:, D * b + HALF * h:D * b + HALF * h + HALF],
                                          start=(k == 0), stop=(k == KT - 1))
                        last.then_inc(gu_used, 1)
                        if k in (2, 5):
                            if k == 2:
                                pe.wait_ge(yb_ready, i + 1)
                            pe.wait_ge(added, 3 * i + (k // 3 + 3))
                            scatter(k // 3)
                    pe.wait_ge(pick_ready, i + 2)
                    gather()
                    pe.wait_ge(gate_kept, i + 1)
                    for j in range(CH):
                        last = nc.tensor.transpose(PS[:, 2, P * j:P * j + P], hgu[:, P * j:P * j + P], ident[:])
                    last.then_inc(gate_turned, 1)
                    pe.wait_ge(up_kept, i + 1)
                    for j in range(CH):
                        last = nc.tensor.transpose(PS[:, 3, P * j:P * j + P], hgu[:, HALF + P * j:HALF + P * j + P],
                                                   ident[:])
                    last.then_inc(up_turned, 1)
                    pe.wait_ge(added, 3 * i + 5)
                    scatter(2)
                    pe.wait_ge(pick_gate_ready, i + 1)
                    for t in range(NT):
                        last = nc.tensor.transpose(PS[:, 4, P * t:P * t + P], pick_gate[:, t, :], ident[:])
                    last.then_inc(spread_turned, 1)
                    pe.wait_ge(spread_ready, i + 1)
                    pe.wait_ge(act_ready, i + 1)
                    for f in range(KT):
                        if f % 2 == 0:
                            pe.wait_ge(down_landed[f // 2], 16 * i + 16)
                        for h in range(2):
                            last = mm(PS[SLOTS * h:SLOTS * h + SLOTS, 4, :], actT[:, f % 4, f // 4, :],
                                      down_ring[:, f, HALF * h:HALF * h + HALF], start=(f == 0), stop=(f == KT - 1))
                        if f % 2:
                            last.then_inc(down_used, 1)
            pe.wait_ge(yb_ready, rounds * E + 1)
            for t in range(NT):
                pe.wait_ge(added, rounds * (3 * E) + (t + 3))
                scatter(t)

        @block.vector
        def _(v):
            tt, ts, stt = nc.vector.tensor_tensor, nc.vector.tensor_scalar, nc.vector.scalar_tensor_tensor
            count = [0]

            def step(ins):
                count[0] += 1
                ins.then_inc(dve, 1)
                v.wait_ge(dve, count[0])

            def mark(ins):
                count[0] += 1
                ins.then_inc(dve, 1)

            def done():
                v.wait_ge(dve, count[0])

            mark(nc.vector.memset(stat[:], 1.0))
            mark(nc.vector.memset(XN[:, 2, :], 0.0))
            mark(nc.vector.memset(spread[:], 0.0))
            nc.vector.memset(yb[:], 0.0).then_inc(yb_ready, 1)
            v.wait_ge(rows_turned, 4)
            nc.vector.tensor_copy(params[:], PS[:, 4, 0:24]).then_inc(rows_kept, 1)
            for b in range(2):
                nc.vector.tensor_copy(bias_gu[:, :, b, :, :].rearrange("p e j h -> p h j e"),
                                      PS[:, 5, 256 * b:256 * b + 256].rearrange("p (h j e) -> p h j e", h=2, j=CH)
                                      ).then_inc(rows_kept, 1)
            v.wait_ge(consts, 7)
            nc.vector.tensor_copy(poolT, PS[:, 6, 0:480].rearrange("p (c b r) -> p c b r", c=CH, r=PBUF)
                                  ).then_inc(rows_kept, 1)
            nc.vector.tensor_copy(convT, PS[:, 7, 0:64].rearrange("p (c b r) -> p c b r", c=CH, r=CBUF)
                                  ).then_inc(rows_kept, 1)

            def rstd(n, base):
                v.wait_ge(squared, NT * n + NT)
                done()
                ts(stat[:, 1, :], stat[:, 0, :], 1.0 / D, EPS, ALU.mult, ALU.add).then_inc(normed, 1)
                v.wait_ge(rooted, n + 1)
                step(nc.vector.reciprocal(stat[:, 3, :], stat[:, 2, :]))

            rstd(0, 0)
            for t in range(NT):
                rows = slice(0, P if t < 2 else SAMPLE + META)
                ts(XN[rows, t, :], Y[rows, t, :], stat[rows, 3, t:t + 1], None, ALU.mult).then_inc(normed, 1)
            v.wait_ge(rows_kept, 1)
            for t in range(NT):
                v.wait_ge(x_turned, t + 1)
                if t < 2:
                    for q in range(2):
                        tt(hT[:, 4 * q:4 * q + 4, META + P * t:META + P * t + P],
                           PS[:, 2 * t + q, :].rearrange("p (k t) -> p k t", k=4),
                           params[:, 4 * q:4 * q + 4].unsqueeze(2).to_broadcast([P, 4, P]), ALU.mult).then_inc(h_ready, 1)
                else:
                    src = PS[:, 4, 0:KT * (SAMPLE + META)].rearrange("p (k t) -> p k t", k=KT)
                    tt(hT[:, :, COLS - SAMPLE:COLS], src[:, :, 0:SAMPLE],
                       params[:, 0:8].unsqueeze(2).to_broadcast([P, KT, SAMPLE]), ALU.mult).then_inc(h_ready, 1)
                    tt(hT[:, :, 0:META], src[:, :, SAMPLE:SAMPLE + META],
                       params[:, 0:8].unsqueeze(2).to_broadcast([P, KT, META]), ALU.mult).then_inc(h_ready, 1)

            end = META + PROMPT
            v.wait_ge(z_kept, 4)
            v.wait_ge(rows_kept, 5)
            for g, w in enumerate(WINDOWS):
                src, span, bufs = uT[:, g, :], 1, [scr_a, scr_b]
                while span < w:
                    dst = bufs[0]
                    lo = 2 * span - 1
                    step(tt(dst[:, lo:end], src[:, lo:end], src[:, lo - span:end - span], ALU.add))
                    src, span, bufs = dst, 2 * span, bufs[::-1]
                stt(pmT[:, g, 0:PROMPT], src[:, META:end], 1.0 / w, uT[:, g, META:end], ALU.mult,
                    ALU.subtract).then_inc(dve, 1)
                count[0] += 1
                done()
                step(nc.vector.tensor_reduce(scr_a[:, 0:SAMPLE], poolT[:, g, :, PBUF + 1 - w:PBUF], AXX, ALU.add))
                step(tt(scr_a[:, 0:SAMPLE], scr_a[:, 0:SAMPLE], uT[:, g, end:COLS], ALU.add))
                stt(pmT[:, g, PROMPT:TOK], scr_a[:, 0:SAMPLE], 1.0 / w, uT[:, g, end:COLS], ALU.mult,
                    ALU.subtract).then_inc(pm_ready, 1)
                v.wait_ge(pm_ready, g + 1)

            v.wait_ge(z_kept, 12)
            for c in range(CH):
                v.wait_ge(z_done, 13 + c)
                tt(cvT[:, c, :], PS[:, c, 0:COLS], cT[:, c, :], ALU.mult).then_inc(cv_done, 1)
            for c in range(CH):
                v.wait_ge(cv_done, c + 1)
                tap = [params[:, 12 + 4 * k + c:13 + 4 * k + c] for k in range(CW)]
                acc, accs = scr_a[:, 0:PROMPT], scr_a[:, PROMPT:TOK]
                cv = cvT[:, c, :]
                mark(ts(acc, cv[:, META - 2:end - 2], tap[0], None, ALU.mult))
                step(ts(accs, convT[:, c, :, 0], tap[0], None, ALU.mult))
                mark(stt(acc, cv[:, META - 1:end - 1], tap[1], acc, ALU.mult, ALU.add))
                step(stt(accs, convT[:, c, :, 1], tap[1], accs, ALU.mult, ALU.add))
                mark(stt(acc, cv[:, META:end], tap[2], acc, ALU.mult, ALU.add))
                step(stt(accs, cv[:, end:COLS], tap[2], accs, ALU.mult, ALU.add))
                tt(cbT[:, c, :], scr_a[:, 0:TOK], bT[:, c, :], ALU.mult).then_inc(cb_ready, 1)
                v.wait_ge(cb_ready, c + 1)

            for g in range(CH):
                v.wait_ge(grp_done, g + 1)
                ts(paT[:, g, :], PS[:, 4 + g, 0:TOK], params[:, 8 + g:9 + g], None, ALU.mult).then_inc(pa_ready, 1)

            v.wait_ge(z_kept, 28)
            for m in range(KT):
                v.wait_ge(branches, m + 1)
                mark(tt(mT[:, m, :], PS[:, 4 + 2 * (m % 2), 0:TOK], gatesT[:, m, :], ALU.mult))
                step(tt(scr_a[:, 0:TOK], PS[:, 5 + 2 * (m % 2), 0:TOK], gatesT[:, KT + m, :], ALU.mult))
                tt(mT[:, m, :], mT[:, m, :], scr_a[:, 0:TOK], ALU.add).then_inc(mixed, 1)
                v.wait_ge(mixed, m + 1)

            for t in range(2):
                v.wait_ge(wo_done, 2 * t + 2)
                tt(Y[:, t, :].rearrange("p (h n) -> p h n", h=2), PS[:, 2 * t:2 * t + 2, :],
                   Y[:, t, :].rearrange("p (h n) -> p h n", h=2), ALU.add).then_inc(resid, 1)
            v.wait_ge(samp_staged, 4)
            tt(Y[0:SAMPLE, 2, :], samp_stage, Y[0:SAMPLE, 2, :], ALU.add).then_inc(resid, 1)
            mark(nc.vector.memset(ones, 1.0))
            mark(nc.vector.memset(logits, 0.0))
            mark(nc.vector.memset(valid[:, 0:2], 1.0))
            mark(nc.vector.memset(valid[:, 2:3], 0.0))
            for r in range(1, ROUNDS):
                mark(nc.vector.memset(bounds[:, r - 1:r], float(SLOTS * r)))
            done()
            step(nc.vector.memset(valid[0:SAMPLE, 2:3], 1.0))
            rstd(1, 3)
            v.wait_ge(late_landed, 64)
            for t in range(NT):
                rows = slice(0, P if t < 2 else SAMPLE)
                stt(XN[rows, t, :], Y[rows, t, :], stat[rows, 3, t:t + 1], g_ffn_all[rows, :], ALU.mult,
                    ALU.mult).then_inc(normed, 1)

            v.wait_ge(logits_done, NT)
            for t in range(NT):
                rows = slice(0, P if t < 2 else SAMPLE)
                mark(tt(logits[rows, t, :], PS[rows, 2, E * t:E * t + E], br_all[rows, :], ALU.add))
            done()
            for t in range(NT):
                mark(nc.vector.max(top[:, t, :], logits[:, t, :]))
            done()
            tt(ex, top[:, :, 0:TOPK], top[:, :, 0:1].to_broadcast([P, NT, TOPK]), ALU.subtract).then_inc(shifted, 1)
            for t in range(NT):
                mark(nc.vector.max_index(topi[:, t, :].bitcast(U32), top[:, t, :], logits[:, t, :]))
            done()
            step(nc.vector.tensor_copy(topf, topi.bitcast(U32)))
            for t in range(NT):
                mark(tt(hot[:, t, :, :], slot_no[:, 0:E].unsqueeze(1).to_broadcast([P, TOPK, E]),
                        topf[:, t, 0:TOPK].unsqueeze(2).to_broadcast([P, TOPK, E]), ALU.is_equal))
            done()
            step(nc.vector.tensor_reduce(mask, hot.rearrange("p t k e -> p t e k"), AXX, ALU.add))
            tt(mask, mask, valid.unsqueeze(2).to_broadcast([P, NT, E]), ALU.mult).then_inc(mask_ready, 1)
            v.wait_ge(exped, 1)
            step(nc.vector.tensor_reduce(exs, ex, AXX, ALU.add))
            step(nc.vector.reciprocal(exs, exs))
            step(tt(ex, ex, exs.unsqueeze(2).to_broadcast([P, NT, TOPK]), ALU.mult))
            for t in range(NT):
                mark(tt(hotg[:, t, :, :], hot[:, t, :, :], ex[:, t, :].unsqueeze(2).to_broadcast([P, TOPK, E]),
                        ALU.mult))
            done()
            nc.vector.tensor_reduce(G, hotg.rearrange("p t k e -> p t e k"), AXX, ALU.add).then_inc(mask_ready, 1)
            v.wait_ge(mask_ready, 2)
            v.wait_ge(ranks, 1)
            step(stt(pos1, PS[:, 3, 0:NT * E].rearrange("p (t e) -> p t e", e=E), 1.0, mask, ALU.add, ALU.mult))
            for r in range(ROUNDS):
                mark(ts(table[:, E * r:E * r + E, 0:NT].rearrange("p e t -> p t e"), pos1, -1.0 - SLOTS * r, None,
                        ALU.add))
                mark(nc.vector.tensor_copy(table[:, E * r:E * r + E, NT:2 * NT].rearrange("p e t -> p t e"), G))
            done()
            step(nc.vector.tensor_reduce(most, PS[:, 3, NT * E:NT * E + E], AXX, ALU.max))
            step(tt(over, bounds, most.to_broadcast([P, ROUNDS - 1]), ALU.is_lt))
            step(nc.vector.tensor_reduce(most, over, AXX, ALU.add))
            nc.vector.tensor_scalar(rounds_sb[:], most, 1.0, None, ALU.add).then_inc(rounds_ready, 1)

            def load_item(item, n):
                nc.vector.tensor_copy(cur[:], table[:, item, :] if type(item) is int else
                                      table[:, bass.ds(item, 1), :].rearrange("p a t -> p (a t)")
                                      ).then_inc(cur_ready, 1)
                v.wait_ge(cur_ready, n)

            def make_pick():
                tt(pick[:], slot_no[:].unsqueeze(1).to_broadcast([P, NT, SLOTS]),
                   cur[:, 0:NT].unsqueeze(2).to_broadcast([P, NT, SLOTS]), ALU.is_equal).then_inc(pick_ready, 1)

            load_item(0, 1)
            make_pick()
            for t in range(NT):
                rows = slice(0, P if t < 2 else SAMPLE)
                v.wait_ge(bd_done, t + 1)
                tt(Y[rows, t, :].rearrange("p (h n) -> p h n", h=2), PS[rows, 6:8, :],
                   Y[rows, t, :].rearrange("p (h n) -> p h n", h=2), ALU.add).then_inc(added, 1)
            v.wait_ge(added, 3)
            v.wait_ge(gt_kept, 1)
            v.wait_ge(rounds_ready, 1)
            v.wait_ge(pick_ready, 1)
            rounds = v.value_load(rounds_sb[0:1, 0:1], min_val=1, max_val=ROUNDS)
            nc.vector.memset(spare[:], 0.0).then_inc(rounds_ready, 1)

            def add_rows(t, n):
                rows = slice(0, P if t < 2 else SAMPLE)
                v.wait_ge(scattered, n)
                tt(Y[rows, t, :].rearrange("p (h n) -> p h n", h=2), PS[rows, 6:8, :],
                   Y[rows, t, :].rearrange("p (h n) -> p h n", h=2), ALU.add).then_inc(added, 1)

            with v.Fori(0, rounds) as r:
                with v.Fori(0, E) as e:
                    i = v.snap(r * E + e)
                    v.wait_ge(pick_ready, i + 1)
                    v.wait_ge(gu_used, 8 * i + 1)
                    tt(pick_gate[:, :, 0:SLOTS], pick[:], cur[:, NT:2 * NT].unsqueeze(2).to_broadcast([P, NT, SLOTS]),
                       ALU.mult).then_inc(cur_ready, 1)
                    tt(pick_gate[:, :, SLOTS:2 * SLOTS], pick[:],
                       cur[:, NT:2 * NT].unsqueeze(2).to_broadcast([P, NT, SLOTS]), ALU.mult).then_inc(cur_ready, 1)
                    v.wait_ge(cur_ready, 3 * i + 3)
                    nc.vector.tensor_copy(cur[:], table[:, bass.ds(i + 1, 1), :].rearrange("p a t -> p (a t)")
                                          ).then_inc(cur_ready, 1)
                    nc.vector.memset(spare[:], 0.0).then_inc(pick_gate_ready, 1)
                    v.wait_ge(cur_ready, 3 * i + 4)
                    v.wait_ge(gathered, i + 1)
                    make_pick()
                    add_rows(0, 3 * i + 1)
                    add_rows(1, 3 * i + 2)
                    v.wait_ge(gu_used, 8 * i + 8)
                    nc.vector.tensor_copy(hgu[:, HALF:2 * HALF], PS[:, 1, :]).then_inc(up_kept, 1)

                    def biased(b):
                        tt(hgu[:, HALF * b:HALF * b + HALF].rearrange("p (c s) -> p c s", s=SLOTS),
                           PS[:, 2 + b, :].rearrange("p (c s) -> p c s", s=SLOTS),
                           bias_gu[:, bass.ds(e, 1), b, :, :].rearrange("p a j h -> p (a j h)").unsqueeze(2)
                           .to_broadcast([P, 8, SLOTS]), ALU.add).then_inc((g_biased, u_biased)[b], 1)

                    gate, up = hgu[:, 0:HALF], hgu[:, HALF:2 * HALF]
                    v.wait_ge(gate_turned, i + 1)
                    biased(0)
                    v.wait_ge(g_biased, i + 1)
                    ts(gate, gate, LIMIT, None, ALU.min).then_inc(g_ready, 1)
                    v.wait_ge(up_turned, i + 1)
                    biased(1)
                    v.wait_ge(u_biased, i + 1)
                    ts(up, up, LIMIT, -LIMIT, ALU.min, ALU.max).then_inc(u_ready, 1)
                    v.wait_ge(u_ready, i + 1)
                    v.wait_ge(g_ready, i + 1)
                    stt(up, up, 1.0, gate, ALU.add, ALU.mult).then_inc(gu_product, 1)
                    v.wait_ge(gu_product, i + 1)
                    v.wait_ge(sig_ready, i + 1)
                    tt(actT[:].rearrange("p j h s -> p (j h s)"), up, sig, ALU.mult).then_inc(act_ready, 1)
                    add_rows(2, 3 * i + 3)
            for t in range(NT):
                add_rows(t, rounds * (3 * E) + (t + 1))
            v.wait_ge(squared, 9)
            ts(stat[:, 1, :], stat[:, 0, :], 1.0 / D, EPS, ALU.mult, ALU.add).then_inc(normed, 1)
            v.wait_ge(rooted, 3)
            step(nc.vector.reciprocal(stat[:, 3, :], stat[:, 2, :]))
            v.wait_ge(gfin_landed, 16)
            for t in range(NT):
                rows = slice(0, P if t < 2 else SAMPLE)
                stt(Y[rows, t, :], Y[rows, t, :], stat[rows, 3, t:t + 1], XN[rows, 0, :], ALU.mult,
                    ALU.mult).then_inc(fin, 1)


_INS = ['x_prompt', 'x_sample', 'state_pool', 'state_conv', 'meta_tokens', 'g_mix', 'w_in', 'w_pool_grp', 'pool_scale',
        'w_pool_up', 'w_conv', 'w_conv_out', 'w_o', 'g_ffn', 'w_router', 'b_router', 'w_gu', 'b_gu', 'w_down', 'b_down',
        'g_final']
_OUTS = [((1, PROMPT, D), 'float32'), ((SAMPLE, 1, D), 'float32'), ((1, 1, PBUF, HALF), 'float32'),
         ((1, 1, CBUF, HALF), 'float32'), ((1, SAMPLE, PBUF, HALF), 'float32'), ((1, SAMPLE, CBUF, HALF), 'float32')]


def kernel(**inputs):
    import numpy as _np
    import concourse.bacc as _bacc
    from concourse import mybir as _mybir
    from concourse.bass_utils import run_bass_kernel_spmd as _run

    nc = _bacc.Bacc("TRN2", target_bir_lowering=False, num_devices=1, dynamic_dma_scratch_size=1024)
    arrays, args = {}, []
    for name in _INS:
        a = _np.ascontiguousarray(inputs[name])
        arrays[f"in_{name}_dram"] = a
        args.append(nc.dram_tensor(f"in_{name}_dram", a.shape, _mybir.dt.from_np(a.dtype), kind="ExternalInput").ap())
    for i, (shape, dtype) in enumerate(_OUTS):
        dt = _mybir.dt.from_np(_np.dtype(dtype))
        args.append(nc.dram_tensor(f"out_{i}_dram", shape, dt, kind="ExternalOutput").ap())
    build(nc, *args)
    r = _run(nc, [arrays], core_ids=[0])
    return tuple(r.results[0][f"out_{i}_dram"] for i in range(len(_OUTS)))
```

```python
from contextlib import ExitStack

import concourse.bass as bass
from concourse import mybir

ALU = mybir.AluOpType
ACT = mybir.ActivationFunctionType
AXX = mybir.AxisListType.X
F32 = mybir.dt.float32
F32R = mybir.dt.float32r
I32 = mybir.dt.int32
U32 = mybir.dt.uint32

P = 128
D = 1024
KT = D // P
HALF = 512
CH = HALF // P
META, PROMPT, SAMPLE = 16, 256, 8
TOK = PROMPT + SAMPLE
COLS = META + TOK
NT = 3
WINDOWS = (2, 4, 8, 16)
PBUF, CBUF, CW = 15, 2, 3
E, TOPK = 32, 4
SLOTS = 64
ROUNDS = -(-TOK // SLOTS)
ITEMS = ROUNDS * E
LIMIT, ALPHA, EPS = 7.0, 1.702, 1e-5
LOW_AT = 32
NCHUNK = 32


def build(nc, x_prompt, x_sample, state_pool, state_conv, meta_tokens, g_mix, w_in, w_pool_grp, pool_scale,
          w_pool_up, w_conv, w_conv_out, w_o, g_ffn, w_router, b_router, w_gu, b_gu, w_down, b_down, g_final,
          y_prompt, y_sample, new_pool_prompt, new_conv_prompt, new_pool_sample, new_conv_sample):
    with ExitStack() as ctx:
        def sb(name, shape, dt=F32):
            return ctx.enter_context(nc.sbuf_tensor(name, shape, dt))

        def sem(name):
            return ctx.enter_context(nc.semaphore(name))

        gu_ring = sb("gu_ring", [P, 2 * KT, 2 * D])
        down_ring = sb("down_ring", [P, KT, D])
        Y = sb("Y", [P, NT, D])
        XP = sb("XP", [P, 5, D], F32R)
        work = sb("work", [P, 2112])
        table = sb("table", [P, ITEMS + 2, 2 * NT])
        bias_gu = sb("bias_gu", [P, E, 2, CH, 2])
        ident = sb("ident", [P, P])
        slot_no = sb("slot_no", [P, 2 * SLOTS])
        pick = sb("pick", [P, NT, SLOTS], F32R)
        pick_twice = sb("pick_twice", [P, NT, 2 * SLOTS])
        XgT = sb("XgT", [P, KT, SLOTS])
        spread = sb("spread", [P, NT, P], F32R)
        slot_gate = sb("slot_gate", [P, 1])
        actT = sb("actT", [P, CH, 2, SLOTS])
        y_high = sb("y_high", [P, HALF], F32R)
        y_low = sb("y_low", [P, HALF], F32R)
        params = sb("params", [P, 24])
        cur = sb("cur", [P, 2 * NT])
        cur_back = sb("cur_back", [P, 2 * NT])
        stat = sb("stat", [P, 4, NT])
        more_sb = sb("more_sb", [P, 1], I32)
        PS = ctx.enter_context(nc.psum_tensor("PS", [P, 8, HALF], F32))

        hgu = work[:, 0:1024]
        sig = work[:, 1024:1536]
        poolT = work[:, 0:480].rearrange("p (c b r) -> p c b r", c=CH, r=PBUF)
        convT = work[:, 480:544].rearrange("p (c b r) -> p c b r", c=CH, r=CBUF)
        tail_u = work[:, 544:1056]
        tail_cv = work[:, 1056:1568]
        scr_a = work[:, 1568:1840]
        scr_b = work[:, 1840:2112]
        xn2T = work[:, 0:KT * TOK].rearrange("p (k t) -> p k t", t=TOK)

        g_fin_all = gu_ring[:, 2, 0:D]
        low = gu_ring[:, KT:2 * KT, :].rearrange("p k n -> p (k n)")
        hT = low[:, 0:2240].rearrange("p (k t) -> p k t", t=COLS)
        uT = low[:, 2240:3360].rearrange("p (k t) -> p k t", t=COLS)
        cT = low[:, 3360:4480].rearrange("p (k t) -> p k t", t=COLS)
        bT = low[:, 4480:5536].rearrange("p (k t) -> p k t", t=TOK)
        cvT = low[:, 5536:6656].rearrange("p (k t) -> p k t", t=COLS)
        gatesT = low[:, 6656:10880].rearrange("p (k t) -> p k t", t=TOK)
        pmT = low[:, 10880:11936].rearrange("p (k t) -> p k t", t=TOK)
        paT = low[:, 11936:12992].rearrange("p (k t) -> p k t", t=TOK)
        cbT = low[:, 12992:14048].rearrange("p (k t) -> p k t", t=TOK)
        mT = low[:, 14048:16160].rearrange("p (k t) -> p k t", t=TOK)
        below = low[:, 16160:16288]
        bgu_rows = low[0:E, 6656:8704]
        pool_rows = low[0:SAMPLE * PBUF, 8704:9216]
        conv_rows = low[0:SAMPLE * CBUF, 9216:9728]
        param_rows = low[0:24, 9728:9856]
        grp = low[:, 14048:14560].rearrange("p (g d) -> p g d", g=CH)
        spare = sb("spare", [P, 1])
        XN1 = low[:, 10880:13952].rearrange("p (t n) -> p t n", t=NT)
        XN2 = low[:, 6656:9728].rearrange("p (t n) -> p t n", t=NT)
        g_ffn_all = low[:, 0:1024]
        bdown_rows = low[0:E, 1024:2048]
        wr = low[:, 3360:3616].rearrange("p (k e) -> p k e", e=E)
        br_all = low[:, 3616:3648]
        samp_stage = low[0:SAMPLE, 10880:11904]
        rt = 4480

        def route(n):
            nonlocal rt
            rt += n
            assert rt <= 6656
            return low[:, rt - n:rt]

        ones = route(P)
        logits = route(NT * E).rearrange("p (t e) -> p t e", e=E)
        top = route(NT * 8).rearrange("p (t e) -> p t e", e=8)
        topi = route(NT * 8).rearrange("p (t e) -> p t e", e=8)
        topf = route(NT * 8).rearrange("p (t e) -> p t e", e=8)
        ex = route(NT * TOPK).rearrange("p (t e) -> p t e", e=TOPK)
        exs = route(NT)
        valid = route(NT)
        hot = route(NT * TOPK * E).rearrange("p (t k e) -> p t k e", k=TOPK, e=E)
        hotg = route(NT * TOPK * E).rearrange("p (t k e) -> p t k e", k=TOPK, e=E)
        mask = route(NT * E).rearrange("p (t e) -> p t e", e=E)
        G = route(NT * E).rearrange("p (t e) -> p t e", e=E)
        pos1 = route(NT * E).rearrange("p (t e) -> p t e", e=E)
        GT = route(TOK)
        most = route(1)
        over = route(ROUNDS - 1)
        bounds = route(ROUNDS - 1)

        pool_up = gu_ring[:, 0:2, :].rearrange("p s n -> p (s n)").rearrange("p (k n) -> p k n", k=CH)
        conv_out = gu_ring[:, 2:4, :].rearrange("p s n -> p (s n)").rearrange("p (k n) -> p k n", k=CH)

        win_landed = [sem(f"win_landed{s}") for s in range(KT)]
        x_landed = sem("x_landed")
        rows_landed = sem("rows_landed")
        grp_landed = sem("grp_landed")
        up_landed = sem("up_landed")
        convout_landed = sem("convout_landed")
        wo_landed = sem("wo_landed")
        late_landed = sem("late_landed")
        consts = sem("consts")
        rows_turned = sem("rows_turned")
        rows_kept = sem("rows_kept")
        squared = sem("squared")
        rooted = sem("rooted")
        normed = sem("normed")
        x_turned = sem("x_turned")
        h_ready = sem("h_ready")
        z_done = sem("z_done")
        z_kept = sem("z_kept")
        cv_done = sem("cv_done")
        dve = sem("dve")
        cb_ready = sem("cb_ready")
        pm_ready = sem("pm_ready")
        tails_turned = sem("tails_turned")
        tails_kept = sem("tails_kept")
        grp_done = sem("grp_done")
        pa_ready = sem("pa_ready")
        branches = sem("branches")
        mixed = sem("mixed")
        wo_done = sem("wo_done")
        samp_staged = sem("samp_staged")
        resid = sem("resid")
        x2_turned = sem("x2_turned")
        x2_kept = sem("x2_kept")
        logits_done = sem("logits_done")
        shifted = sem("shifted")
        exped = sem("exped")
        mask_ready = sem("mask_ready")
        ranks = sem("ranks")
        gt_turned = sem("gt_turned")
        gt_kept = sem("gt_kept")
        bd_done = sem("bd_done")
        more_ready = sem("more_ready")
        stored = sem("stored")
        gu_landed = [sem(f"gu_landed{s}") for s in range(2 * KT)]
        down_landed = [sem(f"down_landed{q}") for q in range(CH)]
        gu_used = sem("gu_used")
        down_used = sem("down_used")
        pick_ready = sem("pick_ready")
        twice_ready = sem("twice_ready")
        gathered = sem("gathered")
        xg_ready = sem("xg_ready")
        spread_turned = sem("spread_turned")
        spread_ready = sem("spread_ready")
        gate_kept = sem("gate_kept")
        up_kept = sem("up_kept")
        gate_turned = sem("gate_turned")
        up_turned = sem("up_turned")
        cur_ready = sem("cur_ready")
        back_ready = sem("back_ready")
        g_biased = sem("g_biased")
        g_ready = sem("g_ready")
        u_biased = sem("u_biased")
        u_ready = sem("u_ready")
        sig_ready = sem("sig_ready")
        gu_product = sem("gu_product")
        act_ready = sem("act_ready")
        high_ready = sem("high_ready")
        low_ready = sem("low_ready")
        scattered = sem("scattered")
        added = sem("added")
        gfin_landed = sem("gfin_landed")
        fin = sem("fin")

        block = ctx.enter_context(nc.Block())

        def z_evacuated(pe, n):
            if n < 12:
                pe.wait_ge(z_kept, n + 1)
            elif n < 16:
                pe.wait_ge(cv_done, n - 11)
            else:
                pe.wait_ge(z_kept, n - 3)

        @block.sync
        def _(sp):
            sp.dma_start(param_rows[0:8, :], g_mix[0].rearrange("(k p) -> k p", p=P)).then_inc(rows_landed, 16)
            sp.dma_start(param_rows[8:12, :], pool_scale[0].rearrange("(k p) -> k p", p=P)).then_inc(rows_landed, 16)
            sp.dma_start(param_rows[12:24, :], w_conv[0].rearrange("w (k p) -> (w k) p", p=P)
                         ).then_inc(rows_landed, 16)
            sp.dma_start(bgu_rows, b_gu[0]).then_inc(rows_landed, 16)
            sp.dma_start(pool_rows, state_pool[0].rearrange("b r d -> (b r) d")).then_inc(rows_landed, 16)
            sp.dma_start(conv_rows, state_conv[0].rearrange("b r d -> (b r) d")).then_inc(rows_landed, 16)
            for n in range(16):
                if n == 8:
                    sp.dma_start(down_ring[:], w_o[0].rearrange("(k p) n -> p k n", p=P)).then_inc(wo_landed, 16)
                if n >= 8:
                    sp.wait_ge(z_done, 2 * (n - 8) + 2)
                sp.dma_start(gu_ring[:, n % 8, :].rearrange("p (k n) -> p k n", k=KT),
                             w_in[0, :, 256 * n:256 * n + 256].rearrange("(k p) n -> p k n", p=P)
                             ).then_inc(win_landed[n % 8], 16)
            sp.wait_ge(z_done, 20)
            sp.dma_start(pool_up, w_pool_up[0].rearrange("(k p) n -> p k n", p=P)).then_inc(up_landed, 16)
            sp.wait_ge(z_done, 24)
            sp.dma_start(conv_out, w_conv_out[0].rearrange("(k p) n -> p k n", p=P)).then_inc(convout_landed, 16)

            def load_gu(e, parity, k, dynamic):
                src = w_gu[0, bass.ds(e, 1), k * P:(k + 1) * P, :].rearrange("a p n -> (a p) n") if dynamic \
                    else w_gu[0, e, k * P:(k + 1) * P, :]
                sp.dma_start(gu_ring[:, KT * parity + k, :], src).then_inc(gu_landed[KT * parity + k], 16)

            def load_down(e, q, dynamic):
                src = w_down[0, bass.ds(e, 1), 2 * q * P:(2 * q + 2) * P, :].rearrange("a (k p) n -> p (a k) n", p=P) \
                    if dynamic else w_down[0, e, 2 * q * P:(2 * q + 2) * P, :].rearrange("(k p) n -> p k n", p=P)
                sp.dma_start(down_ring[:, 2 * q:2 * q + 2, :], src).then_inc(down_landed[q], 16)

            for k in (4, 5, 6, 7, 0, 1, 2, 3):
                if k >= 4:
                    sp.wait_ge(z_done, 2 * (8 + k) + 2)
                else:
                    sp.wait_ge(branches, 8)
                load_gu(0, 0, k, False)
            sp.wait_ge(wo_done, 5)
            for q in range(CH):
                load_down(0, q, False)
            sp.wait_ge(bd_done, NT)
            sp.wait_ge(more_ready, 2)
            for k in range(KT):
                load_gu(1, 1, k, False)

            def item_down(i, e):
                for q in range(CH):
                    sp.wait_ge(down_used, 4 * i + (q - 3))
                    load_down(e, q, True)

            def item_gu(i, e, parity):
                for k in range(KT):
                    sp.wait_ge(gu_used, 8 * i + (k - 15))
                    load_gu(e, parity, k, True)

            with sp.Fori(0, E // 2 - 1) as pair:
                i = sp.snap(2 * pair + 1)
                e1 = sp.snap(2 * pair + 2)
                e2 = sp.snap(2 * pair + 3)
                item_gu(i + 1, e1, 0)
                item_down(i, i)
                item_gu(i + 2, e2, 1)
                item_down(i + 1, e1)
            for q in range(CH):
                sp.wait_ge(down_used, 4 * (E - 1) + q - 3)
                load_down(E - 1, q, False)

            more = sp.value_load(more_sb[0:1, 0:1], min_val=0, max_val=ROUNDS - 1)
            with sp.If(more > 0):
                with sp.Fori(1, more + 1) as r:
                    with sp.Fori(0, E // 2) as pair:
                        for u in range(2):
                            eu = sp.snap(2 * pair + u)
                            i = sp.snap(r * E + eu)
                            item_gu(i, eu, u)
                            item_down(i, eu)
            sp.wait_ge(gu_used, more * (8 * E) + 8 * (E - 1))
            sp.dma_start(g_fin_all, g_final.rearrange("(a n) -> a n", a=1).to_broadcast([P, D])
                         ).then_inc(gfin_landed, 16)
            for t in range(2):
                sp.wait_ge(fin, t + 1)
                sp.dma_start(y_prompt[0, t * P:(t + 1) * P, :], Y[:, t, :]).then_inc(stored, 16)
            sp.wait_ge(fin, 3)
            sp.dma_start(y_sample[:, 0, :], Y[0:SAMPLE, 2, :]).then_inc(stored, 16)
            sp.wait_ge(stored, 16 * 9)

        @block.gpsimd
        def _(pool):
            nc.gpsimd.memset(ident[:], 0.0).then_inc(consts, 1)
            nc.gpsimd.memset(below, 1.0).then_inc(consts, 1)
            nc.gpsimd.memset(table[:], -1.0).then_inc(consts, 1)
            nc.gpsimd.iota(scr_a.bitcast(I32)[:, 0:2 * SLOTS], pattern=[[0, 2], [1, SLOTS]], base=0,
                           channel_multiplier=0).then_inc(consts, 1)
            pool.wait_ge(consts, 4)
            nc.gpsimd.memset(table[:, :, NT:2 * NT], 0.0).then_inc(consts, 1)
            nc.gpsimd.affine_select(out=ident[:], in_=ident[:], compare_op=ALU.not_equal, fill=1.0, base=0,
                                    pattern=[[-1, P]], channel_multiplier=1).then_inc(consts, 1)
            nc.gpsimd.affine_select(out=below, in_=below, compare_op=ALU.is_gt, fill=0.0, base=0,
                                    pattern=[[1, P]], channel_multiplier=-1).then_inc(consts, 1)
            nc.gpsimd.tensor_copy(slot_no[:], scr_a.bitcast(I32)[:, 0:2 * SLOTS]).then_inc(consts, 1)

        @block.scalar
        def _(act):
            act.dma_start(Y[:, 0, :], x_prompt[0, 0:P, :]).then_inc(x_landed, 16)
            act.dma_start(Y[:, 1, :], x_prompt[0, P:2 * P, :]).then_inc(x_landed, 16)
            act.dma_start(Y[0:SAMPLE, 2, :], x_sample[:, 0, :]).then_inc(x_landed, 16)
            act.dma_start(Y[SAMPLE:SAMPLE + META, 2, :], meta_tokens).then_inc(x_landed, 16)
            def sum_squares(t, rows, squares):
                nc.scalar.activation(squares, Y[rows, t, :], ACT.Square,
                                     accum_out=stat[rows, 0, t:t + 1]).then_inc(squared, 1)

            act.wait_ge(x_landed, 64)
            act.wait_ge(dve, 2)
            for t in range(NT):
                rows = slice(0, P if t < 2 else SAMPLE + META)
                sum_squares(t, rows, XN1[rows, t, :])
            act.wait_ge(normed, 1)
            nc.scalar.activation(stat[:, 2, :], stat[:, 1, :], ACT.Sqrt).then_inc(rooted, 1)

            act.dma_start(grp, w_pool_grp[0].rearrange("g c d -> c g d")).then_inc(grp_landed, 16)
            act.dma_start(new_pool_sample[0, :, 0:PBUF - 1, :], state_pool[0, :, 1:PBUF, :]).then_inc(stored, 16)
            act.dma_start(new_conv_sample[0, :, 0:CBUF - 1, :], state_conv[0, :, 1:CBUF, :]).then_inc(stored, 16)

            for n in range(12):
                dst, cols = ((uT, COLS), (cT, COLS), (bT, TOK))[n // 4]
                act.wait_ge(z_done, n + 1)
                nc.scalar.activation(dst[:, n % 4, :], PS[:, n % 4, 0:cols], ACT.Copy).then_inc(z_kept, 1)
            for n in range(16, 32):
                act.wait_ge(z_done, n + 1)
                nc.scalar.activation(gatesT[:, n - 16, :], PS[:, n % 4, 0:TOK], ACT.Sigmoid).then_inc(z_kept, 1)
                if n == 19:
                    act.wait_ge(tails_turned, 2)
                    nc.scalar.activation(tail_u[0:PBUF + SAMPLE, :], PS[0:PBUF + SAMPLE, 5, :],
                                         ACT.Copy).then_inc(tails_kept, 1)
                    nc.scalar.activation(tail_cv[0:CBUF + SAMPLE, :], PS[0:CBUF + SAMPLE, 6, :],
                                         ACT.Copy).then_inc(tails_kept, 1)
                    act.wait_ge(tails_kept, 2)
                    act.dma_start(new_pool_prompt[0, 0], tail_u[0:PBUF, :]).then_inc(stored, 16)
                    act.dma_start(new_pool_sample[0, :, PBUF - 1, :], tail_u[PBUF:PBUF + SAMPLE, :]
                                  ).then_inc(stored, 16)
                    act.dma_start(new_conv_prompt[0, 0], tail_cv[0:CBUF, :]).then_inc(stored, 16)
                    act.dma_start(new_conv_sample[0, :, CBUF - 1, :], tail_cv[CBUF:CBUF + SAMPLE, :]
                                  ).then_inc(stored, 16)
            act.wait_ge(z_done, 32)
            act.dma_start(g_ffn_all, g_ffn.to_broadcast([P, D])).then_inc(late_landed, 16)
            act.dma_start(bdown_rows, b_down[0]).then_inc(late_landed, 16)
            act.wait_ge(cv_done, 4)
            act.dma_start(wr, w_router[0].rearrange("(k p) e -> p k e", p=P)).then_inc(late_landed, 16)
            act.dma_start(br_all, b_router.to_broadcast([P, E])).then_inc(late_landed, 16)

            act.wait_ge(wo_done, 5)
            for q in range(4):
                nc.scalar.activation(samp_stage[:, 256 * q:256 * q + 256], PS[32 * q:32 * q + SAMPLE, 4, 0:256],
                                     ACT.Copy).then_inc(samp_staged, 1)
            for t in range(NT):
                act.wait_ge(resid, t + 1)
                rows = slice(0, P if t < 2 else SAMPLE)
                sum_squares(t, rows, XN2[rows, t, :])
            act.wait_ge(normed, 5)
            nc.scalar.activation(stat[:, 2, :], stat[:, 1, :], ACT.Sqrt).then_inc(rooted, 1)
            act.wait_ge(stored, 16 * 6)
            for t in range(NT):
                act.wait_ge(x2_turned, t + 1)
                if t < 2:
                    for q in range(2):
                        bank = (5 + 2 * t + q) % 8
                        nc.scalar.activation(xn2T[:, 4 * q:4 * q + 4, P * t:P * t + P],
                                             PS[:, bank, :].rearrange("p (k t) -> p k t", k=4),
                                             ACT.Copy).then_inc(x2_kept, 1)
                else:
                    nc.scalar.activation(xn2T[:, :, 2 * P:TOK],
                                         PS[:, 1, 0:KT * SAMPLE].rearrange("p (k t) -> p k t", k=KT),
                                         ACT.Copy).then_inc(x2_kept, 1)
            act.wait_ge(shifted, 1)
            nc.scalar.activation(ex, ex, ACT.Exp).then_inc(exped, 1)
            act.wait_ge(gt_turned, 1)
            nc.scalar.activation(GT[0:E, :], PS[0:E, 4, 0:TOK], ACT.Copy).then_inc(gt_kept, 1)

            def keep_gathered(count):
                act.wait_ge(gathered, count)
                nc.scalar.activation(XgT[:].rearrange("p k s -> p (k s)"), PS[:, 5, :], ACT.Copy).then_inc(xg_ready, 1)

            keep_gathered(1)
            act.wait_ge(more_ready, 2)
            more = act.value_load(more_sb[0:1, 0:1], min_val=0, max_val=ROUNDS - 1)

            def back(i):
                act.wait_ge(spread_turned, i + 1)
                nc.scalar.activation(spread[:].rearrange("p t s -> p (t s)"), PS[:, 4, 0:NT * P],
                                     ACT.Copy).then_inc(spread_ready, 1)
                nc.scalar.activation(slot_gate[:], PS[:, 4, NT * P:NT * P + 1], ACT.Copy).then_inc(spread_ready, 1)

            def high(i):
                act.wait_ge(down_used, 4 * i + 4)
                act.wait_ge(spread_ready, 2 * i + 2)
                nc.scalar.activation(y_high[:], PS[:, 4, :], ACT.Copy, scale=slot_gate[:]).then_inc(high_ready, 1)

            def sigmoid(i):
                act.wait_ge(g_ready, i + 1)
                nc.scalar.activation(sig, hgu[:, 0:HALF], ACT.Sigmoid, scale=ALPHA).then_inc(sig_ready, 1)

            def item(i, first, before=0):
                if not first:
                    sigmoid(before)
                act.wait_ge(gu_used, 8 * i + 8)
                if not first:
                    act.wait_ge(act_ready, before + 1)
                nc.scalar.activation(hgu[:, 0:HALF], PS[:, 0, :], ACT.Copy).then_inc(gate_kept, 1)
                if not first:
                    back(before)
                keep_gathered(i + 2)
                if not first:
                    high(before)

            item(0, True)
            item(1, False)
            with act.Fori(0, more * E + (E - 2)) as m:
                item(m + 2, False, m + 1)
            last = more * E + (E - 1)
            sigmoid(last)
            back(last)
            high(last)
            for t in range(NT):
                act.wait_ge(added, more * (3 * E) + (3 * E + t + 1))
                rows = slice(0, P if t < 2 else SAMPLE)
                sum_squares(t, rows, gu_ring[rows, 3 + t, 0:D])
            act.wait_ge(normed, 9)
            nc.scalar.activation(stat[:, 2, :], stat[:, 1, :], ACT.Sqrt).then_inc(rooted, 1)

        @block.tensor
        def _(pe):
            mm = nc.tensor.matmul
            pe.wait_ge(consts, 8)
            pe.wait_ge(rows_landed, 96)
            nc.tensor.transpose(PS[:, 4, 0:24], param_rows, ident[0:24, 0:24]).then_inc(rows_turned, 1)
            for c in range(16):
                last = nc.tensor.transpose(PS[:, 5, E * c:E * c + E], bgu_rows[:, P * c:P * c + P], ident[0:E, 0:E])
            last.then_inc(rows_turned, 1)
            n = SAMPLE * PBUF
            for c in range(CH):
                last = nc.tensor.transpose(PS[:, 6, n * c:n * c + n], pool_rows[:, P * c:P * c + P], ident[0:n, 0:n])
            last.then_inc(rows_turned, 1)
            n = SAMPLE * CBUF
            for c in range(CH):
                last = nc.tensor.transpose(PS[:, 7, n * c:n * c + n], conv_rows[:, P * c:P * c + P], ident[0:n, 0:n])
            last.then_inc(rows_turned, 1)

            pe.wait_ge(rows_kept, 1)
            for t in range(NT):
                pe.wait_ge(normed, 2 + t)
                rows = P if t < 2 else SAMPLE + META
                for k in range(KT):
                    out = PS[:, 2 * t + k // 4, P * (k % 4):P * (k % 4) + P] if t < 2 else PS[:, 4, rows * k:rows * k + rows]
                    last = nc.tensor.transpose(out, XN1[0:rows, t, P * k:P * k + P], ident[0:rows, 0:rows])
                last.then_inc(x_turned, 1)

            pe.wait_ge(h_ready, 6)
            for n in range(NCHUNK):
                lo = 0 if n < 8 or 12 <= n < 16 else META
                b = n // 2
                if n % 2 == 0:
                    pe.wait_ge(win_landed[b % 8], 16 * (b // 8 + 1))
                if n >= 4:
                    z_evacuated(pe, n - 4)
                w = gu_ring[:, b % 8, :].rearrange("p (k n) -> p k n", k=KT)
                for k in range(KT):
                    last = mm(PS[:, n % 4, 0:COLS - lo], w[:, k, P * (n % 2):P * (n % 2) + P], hT[:, k, lo:COLS],
                              start=(k == 0), stop=(k == KT - 1))
                last.then_inc(z_done, 1)
                if n == 17:
                    pe.wait_ge(cv_done, 4)
                    pe.wait_ge(rows_kept, 5)
                    for c in range(CH):
                        last = nc.tensor.transpose(PS[0:PBUF + SAMPLE, 5, P * c:P * c + P],
                                                   uT[:, c, COLS - SAMPLE - PBUF:COLS], ident[:])
                    last.then_inc(tails_turned, 1)
                    for c in range(CH):
                        last = nc.tensor.transpose(PS[0:CBUF + SAMPLE, 6, P * c:P * c + P],
                                                   cvT[:, c, COLS - SAMPLE - CBUF:COLS], ident[:])
                    last.then_inc(tails_turned, 1)

            pe.wait_ge(tails_kept, 2)
            pe.wait_ge(pm_ready, 4)
            pe.wait_ge(grp_landed, 16)
            for g in range(CH):
                mm(PS[:, 4 + g, 0:TOK], grp[:, g, :], pmT[:, g, :], start=True, stop=True).then_inc(grp_done, 1)

            pe.wait_ge(pa_ready, 4)
            pe.wait_ge(cb_ready, 4)
            pe.wait_ge(up_landed, 16)
            pe.wait_ge(convout_landed, 16)
            for m in range(KT):
                if m >= 2:
                    pe.wait_ge(mixed, m - 1)
                for k in range(CH):
                    mm(PS[:, 4 + 2 * (m % 2), 0:TOK], pool_up[:, k, P * m:P * m + P], paT[:, k, :],
                       start=(k == 0), stop=(k == CH - 1))
                for k in range(CH):
                    last = mm(PS[:, 5 + 2 * (m % 2), 0:TOK], conv_out[:, k, P * m:P * m + P], cbT[:, k, :],
                              start=(k == 0), stop=(k == CH - 1))
                last.then_inc(branches, 1)

            pe.wait_ge(mixed, 8)
            pe.wait_ge(wo_landed, 16)
            pe.wait_ge(z_kept, 28)
            for t in range(2):
                for h in range(2):
                    for k in range(KT):
                        last = mm(PS[:, 2 * t + h, :], mT[:, k, P * t:P * t + P],
                                  down_ring[:, k, HALF * h:HALF * h + HALF], start=(k == 0), stop=(k == KT - 1))
                    last.then_inc(wo_done, 1)
            for k in range(KT):
                for q in range(4):
                    last = mm(PS[32 * q:32 * q + SAMPLE, 4, 0:256], mT[:, k, 2 * P:TOK],
                              down_ring[:, k, 256 * q:256 * q + 256], start=(k == 0), stop=(k == KT - 1))
            last.then_inc(wo_done, 1)

            pe.wait_ge(late_landed, 64)
            for t in range(NT):
                pe.wait_ge(normed, 6 + t)
                rows = P if t < 2 else SAMPLE
                for k in range(KT):
                    bank = (5 + 2 * t + k // 4) % 8
                    out = PS[:, bank, P * (k % 4):P * (k % 4) + P] if t < 2 else PS[:, 1, rows * k:rows * k + rows]
                    last = nc.tensor.transpose(out, XN2[0:rows, t, P * k:P * k + P], ident[0:rows, 0:rows])
                last.then_inc(x2_turned, 1)
            for t in range(NT):
                pe.wait_ge(x2_kept, (2, 4, 5)[t])
                rows = P if t < 2 else SAMPLE
                for k in range(KT):
                    last = mm(PS[0:rows, 2, E * t:E * t + E], xn2T[:, k, P * t:P * t + rows], wr[:, k, :],
                              start=(k == 0), stop=(k == KT - 1))
                last.then_inc(logits_done, 1)

            pe.wait_ge(mask_ready, 1)
            for t in range(NT):
                for s in range(t + 1):
                    mm(PS[:, 3, E * t:E * t + E], below if s == t else ones, mask[:, s, :],
                       start=(s == 0), stop=(s == t))
            for s in range(NT):
                last = mm(PS[:, 3, E * NT:E * NT + E], ones, mask[:, s, :], start=(s == 0), stop=(s == NT - 1))
            last.then_inc(ranks, 1)
            pe.wait_ge(mask_ready, 2)
            for t in range(NT):
                rows = P if t < 2 else SAMPLE
                last = nc.tensor.transpose(PS[0:E, 4, P * t:P * t + rows], G[0:rows, t, :], ident[0:rows, 0:rows])
            last.then_inc(gt_turned, 1)

            def gather():
                parts = ((0, 0), (2, 0), (1, 1), (3, 1), (4, 2))
                for k in range(KT):
                    for n, (part, t) in enumerate(parts):
                        last = mm(PS[:, 5, SLOTS * k:SLOTS * k + SLOTS], XP[:, part, P * k:P * k + P], pick[:, t, :],
                                  start=(n == 0), stop=(n == len(parts) - 1))
                last.then_inc(gathered, 1)

            def scatter(t):
                for h in range(2):
                    rows = slice(SLOTS * h, SLOTS * h + SLOTS)
                    mm(PS[:, 6 + h, :], spread[rows, t, :], y_high[rows, :], start=True, stop=False)
                    last = mm(PS[:, 6 + h, :], spread[rows, t, :], y_low[rows, :], start=False, stop=True)
                last.then_inc(scattered, 1)

            pe.wait_ge(pick_ready, 1)
            gather()
            pe.wait_ge(gt_kept, 1)
            for t in range(NT):
                rows = P if t < 2 else SAMPLE
                if t:
                    pe.wait_ge(added, t)
                for h in range(2):
                    last = mm(PS[0:rows, 6 + h, :], GT[0:E, P * t:P * t + rows],
                              bdown_rows[:, HALF * h:HALF * h + HALF], start=True, stop=True)
                last.then_inc(bd_done, 1)
            pe.wait_ge(added, 3)
            pe.wait_ge(more_ready, 2)
            more = pe.value_load(more_sb[0:1, 0:1], min_val=0, max_val=ROUNDS - 1)

            def scatter_item(i, t):
                if t == 0:
                    pe.wait_ge(low_ready, i + 1)
                pe.wait_ge(added, 3 * i + (t + 3))
                scatter(t)

            def gate_up(i, u, landed, two_before):
                pe.wait_ge(xg_ready, i + 1)
                for k in range(KT):
                    pe.wait_ge(gu_landed[KT * u + k], landed)
                    w = gu_ring[:, KT * u + k, :]
                    for b in range(2):
                        for h in range(2):
                            last = mm(PS[SLOTS * h:SLOTS * h + SLOTS, b, :], XgT[:, k, :],
                                      w[:, D * b + HALF * h:D * b + HALF * h + HALF],
                                      start=(k == 0), stop=(k == KT - 1))
                    last.then_inc(gu_used, 1)
                    if two_before is not None and k in (2, 4, 6):
                        scatter_item(two_before, k // 2 - 1)

            def way_back(i):
                pe.wait_ge(twice_ready, i + 1)
                for t in range(NT):
                    nc.tensor.transpose(PS[:, 4, P * t:P * t + P], pick_twice[:, t, :], ident[:])
                for t in range(NT):
                    last = mm(PS[:, 4, NT * P:NT * P + 1], pick_twice[:, t, :], cur_back[:, NT + t:NT + t + 1],
                              start=(t == 0), stop=(t == NT - 1))
                last.then_inc(spread_turned, 1)

            def down(i):
                pe.wait_ge(spread_ready, 2 * i + 2)
                pe.wait_ge(act_ready, i + 1)
                for f in range(KT):
                    if f % 2 == 0:
                        pe.wait_ge(down_landed[f // 2], 16 * i + 16)
                    for h in range(2):
                        last = mm(PS[SLOTS * h:SLOTS * h + SLOTS, 4, :], actT[:, f % 4, f // 4, :],
                                  down_ring[:, f, HALF * h:HALF * h + HALF], start=(f == 0), stop=(f == KT - 1))
                    if f % 2:
                        last.then_inc(down_used, 1)

            def turn(i):
                pe.wait_ge(gate_kept, i + 1)
                for j in range(CH):
                    last = nc.tensor.transpose(PS[:, 2, P * j:P * j + P], hgu[:, P * j:P * j + P], ident[:])
                last.then_inc(gate_turned, 1)
                pe.wait_ge(up_kept, i + 1)
                for j in range(CH):
                    last = nc.tensor.transpose(PS[:, 3, P * j:P * j + P], hgu[:, HALF + P * j:HALF + P * j + P],
                                               ident[:])
                last.then_inc(up_turned, 1)

            def item(i, u, landed, before=None, two_before=None):
                gate_up(i, u, landed, two_before)
                if before is not None:
                    way_back(before)
                pe.wait_ge(pick_ready, i + 2)
                gather()
                if before is not None:
                    down(before)
                turn(i)

            item(0, 0, 16)
            item(1, 1, 16, 0)
            with pe.Fori(0, more * (E // 2) + (E // 2 - 1)) as pair:
                item(2 * pair + 2, 0, 16 * pair + 32, 2 * pair + 1, 2 * pair)
                item(2 * pair + 3, 1, 16 * pair + 32, 2 * pair + 2, 2 * pair + 1)
            last, before = more * E + (E - 1), more * E + (E - 2)
            for t in range(NT):
                scatter_item(before, t)
            way_back(last)
            down(last)
            for t in range(NT):
                scatter_item(last, t)

        @block.vector
        def _(v):
            tt, ts, stt = nc.vector.tensor_tensor, nc.vector.tensor_scalar, nc.vector.scalar_tensor_tensor
            count = [0]

            def step(ins):
                count[0] += 1
                ins.then_inc(dve, 1)
                v.wait_ge(dve, count[0])

            def mark(ins):
                count[0] += 1
                ins.then_inc(dve, 1)

            def done():
                v.wait_ge(dve, count[0])

            mark(nc.vector.memset(stat[:], 1.0))
            mark(nc.vector.memset(XP[:, 4, :].bitcast(F32), 0.0))
            v.wait_ge(rows_turned, 4)
            nc.vector.tensor_copy(params[:], PS[:, 4, 0:24]).then_inc(rows_kept, 1)
            for b in range(2):
                nc.vector.tensor_copy(bias_gu[:, :, b, :, :].rearrange("p e j h -> p h j e"),
                                      PS[:, 5, 256 * b:256 * b + 256].rearrange("p (h j e) -> p h j e", h=2, j=CH)
                                      ).then_inc(rows_kept, 1)
            v.wait_ge(consts, 8)
            nc.vector.tensor_copy(poolT, PS[:, 6, 0:480].rearrange("p (c b r) -> p c b r", c=CH, r=PBUF)
                                  ).then_inc(rows_kept, 1)
            nc.vector.tensor_copy(convT, PS[:, 7, 0:64].rearrange("p (c b r) -> p c b r", c=CH, r=CBUF)
                                  ).then_inc(rows_kept, 1)

            def rstd(n, base):
                v.wait_ge(squared, NT * n + NT)
                done()
                ts(stat[:, 1, :], stat[:, 0, :], 1.0 / D, EPS, ALU.mult, ALU.add).then_inc(normed, 1)
                v.wait_ge(rooted, n + 1)
                step(nc.vector.reciprocal(stat[:, 3, :], stat[:, 2, :]))

            rstd(0, 0)
            for t in range(NT):
                rows = slice(0, P if t < 2 else SAMPLE + META)
                ts(XN1[rows, t, :], Y[rows, t, :], stat[rows, 3, t:t + 1], None, ALU.mult).then_inc(normed, 1)
            v.wait_ge(rows_kept, 1)
            for t in range(NT):
                v.wait_ge(x_turned, t + 1)
                if t < 2:
                    for q in range(2):
                        tt(hT[:, 4 * q:4 * q + 4, META + P * t:META + P * t + P],
                           PS[:, 2 * t + q, :].rearrange("p (k t) -> p k t", k=4),
                           params[:, 4 * q:4 * q + 4].unsqueeze(2).to_broadcast([P, 4, P]), ALU.mult).then_inc(h_ready, 1)
                else:
                    src = PS[:, 4, 0:KT * (SAMPLE + META)].rearrange("p (k t) -> p k t", k=KT)
                    tt(hT[:, :, COLS - SAMPLE:COLS], src[:, :, 0:SAMPLE],
                       params[:, 0:8].unsqueeze(2).to_broadcast([P, KT, SAMPLE]), ALU.mult).then_inc(h_ready, 1)
                    tt(hT[:, :, 0:META], src[:, :, SAMPLE:SAMPLE + META],
                       params[:, 0:8].unsqueeze(2).to_broadcast([P, KT, META]), ALU.mult).then_inc(h_ready, 1)

            end = META + PROMPT
            v.wait_ge(z_kept, 4)
            v.wait_ge(rows_kept, 5)
            for g, w in enumerate(WINDOWS):
                src, span, bufs = uT[:, g, :], 1, [scr_a, scr_b]
                while span < w:
                    dst = bufs[0]
                    lo = 2 * span - 1
                    step(tt(dst[:, lo:end], src[:, lo:end], src[:, lo - span:end - span], ALU.add))
                    src, span, bufs = dst, 2 * span, bufs[::-1]
                stt(pmT[:, g, 0:PROMPT], src[:, META:end], 1.0 / w, uT[:, g, META:end], ALU.mult,
                    ALU.subtract).then_inc(dve, 1)
                count[0] += 1
                done()
                step(nc.vector.tensor_reduce(scr_a[:, 0:SAMPLE], poolT[:, g, :, PBUF + 1 - w:PBUF], AXX, ALU.add))
                step(tt(scr_a[:, 0:SAMPLE], scr_a[:, 0:SAMPLE], uT[:, g, end:COLS], ALU.add))
                stt(pmT[:, g, PROMPT:TOK], scr_a[:, 0:SAMPLE], 1.0 / w, uT[:, g, end:COLS], ALU.mult,
                    ALU.subtract).then_inc(pm_ready, 1)
                v.wait_ge(pm_ready, g + 1)

            v.wait_ge(z_kept, 12)
            for c in range(CH):
                v.wait_ge(z_done, 13 + c)
                tt(cvT[:, c, :], PS[:, c, 0:COLS], cT[:, c, :], ALU.mult).then_inc(cv_done, 1)
            for c in range(CH):
                v.wait_ge(cv_done, c + 1)
                tap = [params[:, 12 + 4 * k + c:13 + 4 * k + c] for k in range(CW)]
                acc, accs = scr_a[:, 0:PROMPT], scr_a[:, PROMPT:TOK]
                cv = cvT[:, c, :]
                mark(ts(acc, cv[:, META - 2:end - 2], tap[0], None, ALU.mult))
                step(ts(accs, convT[:, c, :, 0], tap[0], None, ALU.mult))
                mark(stt(acc, cv[:, META - 1:end - 1], tap[1], acc, ALU.mult, ALU.add))
                step(stt(accs, convT[:, c, :, 1], tap[1], accs, ALU.mult, ALU.add))
                mark(stt(acc, cv[:, META:end], tap[2], acc, ALU.mult, ALU.add))
                step(stt(accs, cv[:, end:COLS], tap[2], accs, ALU.mult, ALU.add))
                tt(cbT[:, c, :], scr_a[:, 0:TOK], bT[:, c, :], ALU.mult).then_inc(cb_ready, 1)
                v.wait_ge(cb_ready, c + 1)

            for g in range(CH):
                v.wait_ge(grp_done, g + 1)
                ts(paT[:, g, :], PS[:, 4 + g, 0:TOK], params[:, 8 + g:9 + g], None, ALU.mult).then_inc(pa_ready, 1)

            v.wait_ge(z_kept, 28)
            for m in range(KT):
                v.wait_ge(branches, m + 1)
                mark(tt(mT[:, m, :], PS[:, 4 + 2 * (m % 2), 0:TOK], gatesT[:, m, :], ALU.mult))
                step(tt(scr_a[:, 0:TOK], PS[:, 5 + 2 * (m % 2), 0:TOK], gatesT[:, KT + m, :], ALU.mult))
                tt(mT[:, m, :], mT[:, m, :], scr_a[:, 0:TOK], ALU.add).then_inc(mixed, 1)
                v.wait_ge(mixed, m + 1)

            for t in range(2):
                v.wait_ge(wo_done, 2 * t + 2)
                tt(Y[:, t, :].rearrange("p (h n) -> p h n", h=2), PS[:, 2 * t:2 * t + 2, :],
                   Y[:, t, :].rearrange("p (h n) -> p h n", h=2), ALU.add).then_inc(resid, 1)
            v.wait_ge(samp_staged, 4)
            tt(Y[0:SAMPLE, 2, :], samp_stage, Y[0:SAMPLE, 2, :], ALU.add).then_inc(resid, 1)
            mark(nc.vector.memset(ones, 1.0))
            mark(nc.vector.memset(logits, 0.0))
            mark(nc.vector.memset(valid[:, 0:2], 1.0))
            mark(nc.vector.memset(valid[:, 2:3], 0.0))
            for r in range(1, ROUNDS):
                mark(nc.vector.memset(bounds[:, r - 1:r], float(SLOTS * r)))
            done()
            step(nc.vector.memset(valid[0:SAMPLE, 2:3], 1.0))
            rstd(1, 3)
            v.wait_ge(late_landed, 64)
            for t in range(NT):
                rows = slice(0, P if t < 2 else SAMPLE)
                stt(XN2[rows, t, :], Y[rows, t, :], stat[rows, 3, t:t + 1], g_ffn_all[rows, :], ALU.mult,
                    ALU.mult).then_inc(normed, 1)

            v.wait_ge(normed, 8)
            for t in range(2):
                mark(nc.vector.tensor_copy(XP[:, t, :], XN2[:, t, :]))
            mark(nc.vector.tensor_copy(XP[0:SAMPLE, 4, :], XN2[0:SAMPLE, 2, :]))
            done()
            for t in range(2):
                mark(tt(XP[:, 2 + t, :], XN2[:, t, :], XP[:, t, :].bitcast(F32), ALU.subtract))
            mark(tt(XP[LOW_AT:LOW_AT + SAMPLE, 4, :], XN2[0:SAMPLE, 2, :], XP[0:SAMPLE, 4, :].bitcast(F32),
                    ALU.subtract))

            v.wait_ge(logits_done, NT)
            for t in range(NT):
                rows = slice(0, P if t < 2 else SAMPLE)
                mark(tt(logits[rows, t, :], PS[rows, 2, E * t:E * t + E], br_all[rows, :], ALU.add))
            done()
            for t in range(NT):
                mark(nc.vector.max(top[:, t, :], logits[:, t, :]))
            done()
            tt(ex, top[:, :, 0:TOPK], top[:, :, 0:1].to_broadcast([P, NT, TOPK]), ALU.subtract).then_inc(shifted, 1)
            for t in range(NT):
                mark(nc.vector.max_index(topi[:, t, :].bitcast(U32), top[:, t, :], logits[:, t, :]))
            done()
            step(nc.vector.tensor_copy(topf, topi.bitcast(U32)))
            for t in range(NT):
                mark(tt(hot[:, t, :, :], slot_no[:, 0:E].unsqueeze(1).to_broadcast([P, TOPK, E]),
                        topf[:, t, 0:TOPK].unsqueeze(2).to_broadcast([P, TOPK, E]), ALU.is_equal))
            done()
            step(nc.vector.tensor_reduce(mask, hot.rearrange("p t k e -> p t e k"), AXX, ALU.add))
            tt(mask, mask, valid.unsqueeze(2).to_broadcast([P, NT, E]), ALU.mult).then_inc(mask_ready, 1)
            v.wait_ge(exped, 1)
            step(nc.vector.tensor_reduce(exs, ex, AXX, ALU.add))
            step(nc.vector.reciprocal(exs, exs))
            step(tt(ex, ex, exs.unsqueeze(2).to_broadcast([P, NT, TOPK]), ALU.mult))
            for t in range(NT):
                mark(tt(hotg[:, t, :, :], hot[:, t, :, :], ex[:, t, :].unsqueeze(2).to_broadcast([P, TOPK, E]),
                        ALU.mult))
            done()
            nc.vector.tensor_reduce(G, hotg.rearrange("p t k e -> p t e k"), AXX, ALU.add).then_inc(mask_ready, 1)
            v.wait_ge(mask_ready, 2)
            v.wait_ge(ranks, 1)
            step(stt(pos1, PS[:, 3, 0:NT * E].rearrange("p (t e) -> p t e", e=E), 1.0, mask, ALU.add, ALU.mult))
            for r in range(ROUNDS):
                mark(ts(table[:, E * r:E * r + E, 0:NT].rearrange("p e t -> p t e"), pos1, -1.0 - SLOTS * r, None,
                        ALU.add))
                for t in range(NT):
                    rows = slice(0, P if t < 2 else SAMPLE)
                    mark(nc.vector.tensor_copy(table[rows, E * r:E * r + E, NT + t], G[rows, t, :]))
            done()
            step(nc.vector.tensor_copy(table[LOW_AT:LOW_AT + SAMPLE, :, NT - 1], table[0:SAMPLE, :, NT - 1]))
            step(nc.vector.tensor_reduce(most, PS[:, 3, NT * E:NT * E + E], AXX, ALU.max))
            step(tt(over, bounds, most.to_broadcast([P, ROUNDS - 1]), ALU.is_lt))
            step(nc.vector.tensor_reduce(most, over, AXX, ALU.add))
            nc.vector.tensor_copy(more_sb[:], most).then_inc(more_ready, 1)

            def make_pick(i):
                nc.vector.tensor_copy(cur[:], table[:, i, :] if type(i) is int else
                                      table[:, bass.ds(i, 1), :].rearrange("p a t -> p (a t)")
                                      ).then_inc(cur_ready, 1)
                v.wait_ge(cur_ready, i + 1)
                if type(i) is not int or i > 0:
                    v.wait_ge(gathered, i)
                tt(pick[:], slot_no[:, 0:SLOTS].unsqueeze(1).to_broadcast([P, NT, SLOTS]),
                   cur[:, 0:NT].unsqueeze(2).to_broadcast([P, NT, SLOTS]), ALU.is_equal).then_inc(pick_ready, 1)

            def make_twice(i):
                nc.vector.tensor_copy(cur_back[:], table[:, i, :] if type(i) is int else
                                      table[:, bass.ds(i, 1), :].rearrange("p a t -> p (a t)")
                                      ).then_inc(back_ready, 1)
                v.wait_ge(back_ready, i + 1)
                tt(pick_twice[:], slot_no[:].unsqueeze(1).to_broadcast([P, NT, 2 * SLOTS]),
                   cur_back[:, 0:NT].unsqueeze(2).to_broadcast([P, NT, 2 * SLOTS]), ALU.is_equal
                   ).then_inc(twice_ready, 1)

            make_pick(0)
            for t in range(NT):
                rows = slice(0, P if t < 2 else SAMPLE)
                v.wait_ge(bd_done, t + 1)
                tt(Y[rows, t, :].rearrange("p (h n) -> p h n", h=2), PS[rows, 6:8, :],
                   Y[rows, t, :].rearrange("p (h n) -> p h n", h=2), ALU.add).then_inc(added, 1)
            v.wait_ge(added, 3)
            v.wait_ge(gt_kept, 1)
            v.wait_ge(more_ready, 1)
            v.wait_ge(pick_ready, 1)
            more = v.value_load(more_sb[0:1, 0:1], min_val=0, max_val=ROUNDS - 1)
            nc.vector.memset(spare[:], 0.0).then_inc(more_ready, 1)

            def add_rows(i, t):
                rows = slice(0, P if t < 2 else SAMPLE)
                v.wait_ge(scattered, 3 * i + (t + 1))
                tt(Y[rows, t, :].rearrange("p (h n) -> p h n", h=2), PS[rows, 6:8, :],
                   Y[rows, t, :].rearrange("p (h n) -> p h n", h=2), ALU.add).then_inc(added, 1)

            gate, up = hgu[:, 0:HALF], hgu[:, HALF:2 * HALF]

            def biased(b, e):
                bias = bias_gu[:, e, b, :, :].rearrange("p j h -> p (j h)") if type(e) is int else \
                    bias_gu[:, bass.ds(e, 1), b, :, :].rearrange("p a j h -> p (a j h)")
                tt(hgu[:, HALF * b:HALF * b + HALF].rearrange("p (c s) -> p c s", s=SLOTS),
                   PS[:, 2 + b, :].rearrange("p (c s) -> p c s", s=SLOTS),
                   bias.unsqueeze(2).to_broadcast([P, 8, SLOTS]), ALU.add).then_inc((g_biased, u_biased)[b], 1)

            def swiglu(i, e):
                v.wait_ge(gate_turned, i + 1)
                v.wait_ge(up_turned, i + 1)
                biased(0, e)
                v.wait_ge(g_biased, i + 1)
                ts(gate, gate, LIMIT, None, ALU.min).then_inc(g_ready, 1)
                biased(1, e)
                v.wait_ge(u_biased, i + 1)
                ts(up, up, LIMIT, -LIMIT, ALU.min, ALU.max).then_inc(u_ready, 1)
                v.wait_ge(u_ready, i + 1)
                v.wait_ge(g_ready, i + 1)
                stt(up, up, 1.0, gate, ALU.add, ALU.mult).then_inc(gu_product, 1)
                v.wait_ge(gu_product, i + 1)
                v.wait_ge(sig_ready, i + 1)
                tt(actT[:].rearrange("p j h s -> p (j h s)"), up, sig, ALU.mult).then_inc(act_ready, 1)

            def low_part(i):
                v.wait_ge(high_ready, i + 1)
                stt(y_low[:], PS[:, 4, :], slot_gate[:], y_high[:].bitcast(F32), ALU.mult,
                    ALU.subtract).then_inc(low_ready, 1)

            def item(i, after, before=None, e_before=0, two_before=None):
                if before is not None:
                    swiglu(before, e_before)
                if two_before is not None:
                    for t in range(NT):
                        add_rows(two_before, t)
                if before is not None:
                    make_twice(before)
                make_pick(after)
                v.wait_ge(gu_used, 8 * i + 8)
                if before is not None:
                    v.wait_ge(act_ready, before + 1)
                nc.vector.tensor_copy(up, PS[:, 1, :]).then_inc(up_kept, 1)
                if before is not None:
                    low_part(before)

            item(0, 1)
            item(1, 2, 0)
            with v.Fori(0, more * E + (E - 2)) as m:
                item(m + 2, m + 3, m + 1, (m + 1) % E, m)
            last, before = more * E + (E - 1), more * E + (E - 2)
            make_twice(last)
            swiglu(last, E - 1)
            for t in range(NT):
                add_rows(before, t)
            low_part(last)
            for t in range(NT):
                add_rows(last, t)
            v.wait_ge(squared, 9)
            ts(stat[:, 1, :], stat[:, 0, :], 1.0 / D, EPS, ALU.mult, ALU.add).then_inc(normed, 1)
            v.wait_ge(rooted, 3)
            step(nc.vector.reciprocal(stat[:, 3, :], stat[:, 2, :]))
            v.wait_ge(gfin_landed, 16)
            for t in range(NT):
                rows = slice(0, P if t < 2 else SAMPLE)
                stt(Y[rows, t, :], Y[rows, t, :], stat[rows, 3, t:t + 1], g_fin_all[rows, :], ALU.mult,
                    ALU.mult).then_inc(fin, 1)


_INS = ['x_prompt', 'x_sample', 'state_pool', 'state_conv', 'meta_tokens', 'g_mix', 'w_in', 'w_pool_grp', 'pool_scale',
        'w_pool_up', 'w_conv', 'w_conv_out', 'w_o', 'g_ffn', 'w_router', 'b_router', 'w_gu', 'b_gu', 'w_down', 'b_down',
        'g_final']
_OUTS = [((1, PROMPT, D), 'float32'), ((SAMPLE, 1, D), 'float32'), ((1, 1, PBUF, HALF), 'float32'),
         ((1, 1, CBUF, HALF), 'float32'), ((1, SAMPLE, PBUF, HALF), 'float32'), ((1, SAMPLE, CBUF, HALF), 'float32')]


def kernel(**inputs):
    import numpy as _np
    import concourse.bacc as _bacc
    from concourse import mybir as _mybir
    from concourse.bass_utils import run_bass_kernel_spmd as _run

    nc = _bacc.Bacc("TRN2", target_bir_lowering=False, num_devices=1, dynamic_dma_scratch_size=1024)
    arrays, args = {}, []
    for name in _INS:
        a = _np.ascontiguousarray(inputs[name])
        arrays[f"in_{name}_dram"] = a
        args.append(nc.dram_tensor(f"in_{name}_dram", a.shape, _mybir.dt.from_np(a.dtype), kind="ExternalInput").ap())
    for i, (shape, dtype) in enumerate(_OUTS):
        dt = _mybir.dt.from_np(_np.dtype(dtype))
        args.append(nc.dram_tensor(f"out_{i}_dram", shape, dt, kind="ExternalOutput").ap())
    build(nc, *args)
    r = _run(nc, [arrays], core_ids=[0])
    return tuple(r.results[0][f"out_{i}_dram"] for i in range(len(_OUTS)))
```

```python
from contextlib import ExitStack

import concourse.bass as bass
from concourse import mybir

ALU = mybir.AluOpType
ACT = mybir.ActivationFunctionType
AXX = mybir.AxisListType.X
F32 = mybir.dt.float32
F32R = mybir.dt.float32r
BF16 = mybir.dt.bfloat16
I32 = mybir.dt.int32
U32 = mybir.dt.uint32

P = 128
D = 1024
KT = D // P
HALF = 512
CH = HALF // P
META, PROMPT, SAMPLE = 16, 256, 8
TOK = PROMPT + SAMPLE
COLS = META + TOK
NT = 3
WINDOWS = (2, 4, 8, 16)
PBUF, CBUF, CW = 15, 2, 3
E, TOPK = 32, 4
SLOTS = 64
ROUNDS = -(-TOK // SLOTS)
ITEMS = ROUNDS * E
LIMIT, ALPHA, EPS = 7.0, 1.702, 1e-5
PARTS_AT = (0, 32, 64)
ORDER = (2, 0, 1)
BD_AT = 32
AHEAD = 6
WIN_SLOTS = 6
LAST_BANKS = (6, 0, 2)
NCHUNK = 32


def build(nc, x_prompt, x_sample, state_pool, state_conv, meta_tokens, g_mix, w_in, w_pool_grp, pool_scale,
          w_pool_up, w_conv, w_conv_out, w_o, g_ffn, w_router, b_router, w_gu, b_gu, w_down, b_down, g_final,
          y_prompt, y_sample, new_pool_prompt, new_conv_prompt, new_pool_sample, new_conv_sample):
    with ExitStack() as ctx:
        def sb(name, shape, dt=F32):
            return ctx.enter_context(nc.sbuf_tensor(name, shape, dt))

        def sem(name):
            return ctx.enter_context(nc.semaphore(name))

        with nc.sbuf_tensor("win_low", [P, WIN_SLOTS, 2 * D], F32R) as win_low, \
                nc.sbuf_tensor("win_high", [P, 2, 2 * D], F32R) as win_high, \
                nc.sbuf_tensor("h_high", [P, KT, COLS], F32R) as h_high, \
                nc.sbuf_tensor("rest_of_ring", [P, 8 * 2 * D - KT * COLS], F32), \
                nc.sbuf_tensor("h_low", [P, KT, COLS], F32R) as h_low:
            pass
        gu_ring = sb("gu_ring", [P, 2 * KT, 2 * D])
        down_ring = sb("down_ring", [P, KT, D])
        Y = sb("Y", [P, NT, D])
        XP = sb("XP", [P, 7, D], BF16)
        work = sb("work", [P, 2112])
        table = sb("table", [P, ITEMS + 2, 2 * NT])
        bias_gu = sb("bias_gu", [P, E, 2, CH, 2])
        ident = sb("ident", [P, P])
        slot_no = sb("slot_no", [P, 2 * SLOTS])
        pick = sb("pick", [P, NT, SLOTS], BF16)
        pick_twice = sb("pick_twice", [P, NT, 2 * SLOTS])
        XgT = sb("XgT", [P, KT, SLOTS])
        spread = sb("spread", [P, NT, P], F32R)
        spread_last = sb("spread_last", [P, NT, P], F32R)
        slot_gate = sb("slot_gate", [P, 1])
        actT = sb("actT", [P, CH, 2, SLOTS])
        y_high = sb("y_high", [P, HALF], F32R)
        y_low = sb("y_low", [P, HALF], F32R)
        params = sb("params", [P, 24])
        cur = sb("cur", [P, NT])
        cur_back = sb("cur_back", [P, 2 * NT])
        stat = sb("stat", [P, 4, NT])
        more_sb = sb("more_sb", [P, 1], I32)
        PS = ctx.enter_context(nc.psum_tensor("PS", [P, 8, HALF], F32))

        hgu = work[:, 0:1024]
        sig = work[:, 1024:1536]
        poolT = work[:, 0:480].rearrange("p (c b r) -> p c b r", c=CH, r=PBUF)
        convT = work[:, 480:544].rearrange("p (c b r) -> p c b r", c=CH, r=CBUF)
        tail_u = work[:, 544:1056]
        tail_cv = work[:, 1056:1568]
        scr_a = work[:, 1568:1840]
        scr_b = work[:, 1840:2112]
        xn2T = work[:, 0:KT * TOK].rearrange("p (k t) -> p k t", t=TOK)

        down_last = gu_ring[:, 0:4, :].rearrange("p s (k n) -> p (s k) n", k=2)
        g_fin_all = gu_ring[:, 4, 0:D]
        low = gu_ring[:, KT:2 * KT, :].rearrange("p k n -> p (k n)")
        hT = down_ring[:].rearrange("p k n -> p (k n)")[:, 0:2240].rearrange("p (k t) -> p k t", t=COLS)
        uT = low[:, 2240:3360].rearrange("p (k t) -> p k t", t=COLS)
        cT = low[:, 3360:4480].rearrange("p (k t) -> p k t", t=COLS)
        bT = low[:, 4480:5536].rearrange("p (k t) -> p k t", t=TOK)
        cvT = low[:, 5536:6656].rearrange("p (k t) -> p k t", t=COLS)
        gatesT = low[:, 6656:10880].rearrange("p (k t) -> p k t", t=TOK)
        pmT = low[:, 10880:11936].rearrange("p (k t) -> p k t", t=TOK)
        paT = low[:, 11936:12992].rearrange("p (k t) -> p k t", t=TOK)
        cbT = low[:, 12992:14048].rearrange("p (k t) -> p k t", t=TOK)
        mT = low[:, 14336:16384].rearrange("p (k t) -> p k t", t=PROMPT)
        mT_samp = sb("mT_samp", [P, KT, SAMPLE])
        below = sb("below", [P, P])
        bgu_rows = low[0:E, 6656:8704]
        pool_rows = low[0:SAMPLE * PBUF, 8704:9216]
        conv_rows = low[0:SAMPLE * CBUF, 9216:9728]
        param_rows = low[0:24, 9728:9856]
        grp = low[:, 14336:14848].rearrange("p (g d) -> p g d", g=CH)
        done_mark = sb("done_mark", [P, 1])
        samp_second = sb("samp_second", [SAMPLE, D], BF16)
        XN1 = low[:, 10880:13952].rearrange("p (t n) -> p t n", t=NT)
        g_ffn_all = low[:, 3456:4480]
        XN2 = low[:, 4480:7552].rearrange("p (t n) -> p t n", t=NT)
        samp_stage = work[0:SAMPLE, 0:D]
        wr = sb("wr", [P, KT, E])
        br_all = sb("br_all", [P, E])
        bdown_rows = Y[BD_AT:BD_AT + E, 2, :]
        GT = work[BD_AT:BD_AT + E, 1536:1536 + TOK]
        rt = 2048

        def route(n):
            nonlocal rt
            rt += n
            assert rt <= 3456
            return low[:, rt - n:rt]

        ones = sb("ones", [P, P], BF16)
        below_small = sb("below_small", [P, P], BF16)
        mask_small = sb("mask_small", [P, NT, E], BF16)
        logits = route(NT * E).rearrange("p (t e) -> p t e", e=E)
        top = route(NT * 8).rearrange("p (t e) -> p t e", e=8)
        topi = route(NT * 8).rearrange("p (t e) -> p t e", e=8)
        topf = route(NT * 8).rearrange("p (t e) -> p t e", e=8)
        ex = route(NT * TOPK).rearrange("p (t e) -> p t e", e=TOPK)
        exs = route(NT)
        valid = route(NT)
        hot = route(NT * TOPK * E).rearrange("p (t k e) -> p t k e", k=TOPK, e=E)
        hotg = route(NT * TOPK * E).rearrange("p (t k e) -> p t k e", k=TOPK, e=E)
        mask = route(NT * E).rearrange("p (t e) -> p t e", e=E)
        G = route(NT * E).rearrange("p (t e) -> p t e", e=E)
        pos1 = route(NT * E).rearrange("p (t e) -> p t e", e=E)
        most = route(1)
        over = route(ROUNDS - 1)
        bounds = route(ROUNDS - 1)

        pool_up = gu_ring[:, 4:6, :].rearrange("p s n -> p (s n)").rearrange("p (k n) -> p k n", k=CH)
        conv_out = gu_ring[:, 0:2, :].rearrange("p s n -> p (s n)").rearrange("p (k n) -> p k n", k=CH)

        win_landed = [sem(f"win_landed{s}") for s in range(WIN_SLOTS)]
        x_landed = sem("x_landed")
        rows_landed = sem("rows_landed")
        grp_landed = sem("grp_landed")
        up_landed = sem("up_landed")
        convout_landed = sem("convout_landed")
        wo_landed = sem("wo_landed")
        late_landed = sem("late_landed")
        consts = sem("consts")
        rows_turned = sem("rows_turned")
        rows_kept = sem("rows_kept")
        squared = sem("squared")
        rooted = sem("rooted")
        meaned = sem("meaned")
        normed = sem("normed")
        first_part = sem("first_part")
        first_rest = sem("first_rest")
        second_part = sem("second_part")
        third_part = sem("third_part")
        x_turned = sem("x_turned")
        h_scaled = sem("h_scaled")
        h_rounded = sem("h_rounded")
        h_ready = sem("h_ready")
        win_rounded = sem("win_rounded")
        win_ready = sem("win_ready")
        z_done = sem("z_done")
        z_kept = sem("z_kept")
        cv_done = sem("cv_done")
        dve = sem("dve")
        cb_ready = sem("cb_ready")
        pm_ready = sem("pm_ready")
        tails_turned = sem("tails_turned")
        tails_kept = sem("tails_kept")
        grp_done = sem("grp_done")
        pa_ready = sem("pa_ready")
        branches = sem("branches")
        mixed = sem("mixed")
        wo_done = sem("wo_done")
        samp_staged = sem("samp_staged")
        resid = sem("resid")
        x2_turned = sem("x2_turned")
        x2_kept = sem("x2_kept")
        logits_done = sem("logits_done")
        shifted = sem("shifted")
        exped = sem("exped")
        mask_ready = sem("mask_ready")
        ranks = sem("ranks")
        gt_turned = sem("gt_turned")
        gt_kept = sem("gt_kept")
        bd_done = sem("bd_done")
        more_ready = sem("more_ready")
        stored = sem("stored")
        gu_landed = [sem(f"gu_landed{s}") for s in range(2 * KT)]
        down_landed = [sem(f"down_landed{q}") for q in range(CH)]
        gu_used = sem("gu_used")
        down_used = sem("down_used")
        pick_ready = sem("pick_ready")
        twice_ready = sem("twice_ready")
        gathered = sem("gathered")
        xg_ready = sem("xg_ready")
        spread_turned = sem("spread_turned")
        spread_ready = sem("spread_ready")
        gate_kept = sem("gate_kept")
        up_kept = sem("up_kept")
        gate_turned = sem("gate_turned")
        up_turned = sem("up_turned")
        cur_ready = sem("cur_ready")
        back_ready = sem("back_ready")
        g_biased = sem("g_biased")
        g_ready = sem("g_ready")
        u_biased = sem("u_biased")
        u_ready = sem("u_ready")
        sig_ready = sem("sig_ready")
        gu_product = sem("gu_product")
        act_ready = sem("act_ready")
        high_ready = sem("high_ready")
        low_ready = sem("low_ready")
        scattered = sem("scattered")
        added = sem("added")
        last_landed = [sem(f"last_landed{q}") for q in range(CH)]
        gfin_landed = sem("gfin_landed")
        fin = sem("fin")

        block = ctx.enter_context(nc.Block())

        def h_pieces(h):
            return [h[:, 4 * q:4 * q + 4, META + P * t:META + P * t + P] for t in range(2) for q in range(2)] + \
                [h[:, :, COLS - SAMPLE:COLS], h[:, :, 0:META]]

        def z_evacuated(pe, n):
            if n < 12:
                pe.wait_ge(z_kept, n + 1)
            elif n < 16:
                pe.wait_ge(cv_done, n - 11)
            else:
                pe.wait_ge(z_kept, n - 3)

        @block.sync
        def _(sp):
            sp.dma_start(param_rows[0:8, :], g_mix[0].rearrange("(k p) -> k p", p=P)).then_inc(rows_landed, 16)
            sp.dma_start(param_rows[8:12, :], pool_scale[0].rearrange("(k p) -> k p", p=P)).then_inc(rows_landed, 16)
            sp.dma_start(param_rows[12:24, :], w_conv[0].rearrange("w (k p) -> (w k) p", p=P)
                         ).then_inc(rows_landed, 16)
            sp.dma_start(bgu_rows, b_gu[0]).then_inc(rows_landed, 16)
            sp.dma_start(pool_rows, state_pool[0].rearrange("b r d -> (b r) d")).then_inc(rows_landed, 16)
            sp.dma_start(conv_rows, state_conv[0].rearrange("b r d -> (b r) d")).then_inc(rows_landed, 16)
            for b in range(NCHUNK // 2):
                if b >= WIN_SLOTS:
                    sp.wait_ge(z_done, 2 * (b - WIN_SLOTS) + 2)
                sp.dma_start(gu_ring[:, b % WIN_SLOTS, :].rearrange("p (k n) -> p k n", k=KT),
                             w_in[0, :, 256 * b:256 * b + 256].rearrange("(k p) n -> p k n", p=P)
                             ).then_inc(win_landed[b % WIN_SLOTS], 16)
            sp.wait_ge(z_done, 24)
            sp.dma_start(pool_up, w_pool_up[0].rearrange("(k p) n -> p k n", p=P)).then_inc(up_landed, 16)
            sp.wait_ge(z_done, 28)
            sp.dma_start(conv_out, w_conv_out[0].rearrange("(k p) n -> p k n", p=P)).then_inc(convout_landed, 16)
            sp.wait_ge(z_done, 32)
            sp.dma_start(down_ring[:], w_o[0].rearrange("(k p) n -> p k n", p=P)).then_inc(wo_landed, 16)

            def load_gu(e, parity, k, dynamic):
                src = w_gu[0, bass.ds(e, 1), k * P:(k + 1) * P, :].rearrange("a p n -> (a p) n") if dynamic \
                    else w_gu[0, e, k * P:(k + 1) * P, :]
                sp.dma_start(gu_ring[:, KT * parity + k, :], src).then_inc(gu_landed[KT * parity + k], 16)

            def load_down(e, q, dynamic):
                src = w_down[0, bass.ds(e, 1), 2 * q * P:(2 * q + 2) * P, :].rearrange("a (k p) n -> p (a k) n", p=P) \
                    if dynamic else w_down[0, e, 2 * q * P:(2 * q + 2) * P, :].rearrange("(k p) n -> p k n", p=P)
                sp.dma_start(down_ring[:, 2 * q:2 * q + 2, :], src).then_inc(down_landed[q], 16)

            for k in (2, 3, 6, 7):
                load_gu(0, 0, k, False)
            load_gu(1, 1, 0, False)
            sp.wait_ge(branches, 8)
            for k in (0, 1, 4, 5):
                load_gu(0, 0, k, False)
            sp.wait_ge(mixed, 8)
            for k in (4, 5, 6):
                load_gu(1, 1, k, False)
            sp.wait_ge(wo_done, 5)
            load_gu(1, 1, 7, False)
            for q in range(CH):
                load_down(0, q, False)
            sp.wait_ge(third_part, NT)
            for k in (2, 3):
                load_gu(1, 1, k, False)
            sp.wait_ge(more_ready, 2)
            load_gu(1, 1, 1, False)

            def item_down(i, e):
                for q in range(CH):
                    sp.wait_ge(down_used, 4 * i + (q - 3))
                    load_down(e, q, True)

            def item_gu(i, e, parity):
                for k in range(KT):
                    sp.wait_ge(gu_used, 8 * i + (k - 15))
                    load_gu(e, parity, k, True)

            item_gu(2, 2, 0)
            with sp.Fori(0, AHEAD) as pair:
                i = sp.snap(2 * pair + 1)
                e1 = sp.snap(2 * pair + 2)
                e2 = sp.snap(2 * pair + 3)
                e3 = sp.snap(2 * pair + 4)
                item_gu(i + 2, e2, 1)
                item_down(i, i)
                item_gu(i + 3, e3, 0)
                item_down(i + 1, e1)
            item_down(2 * AHEAD + 1, 2 * AHEAD + 1)
            with sp.Fori(0, E // 2 - 2 - AHEAD) as pair:
                i = sp.snap(2 * pair + (2 * AHEAD + 2))
                e1 = sp.snap(2 * pair + (2 * AHEAD + 3))
                e2 = sp.snap(2 * pair + (2 * AHEAD + 4))
                item_gu(i + 1, e1, 1)
                item_down(i, i)
                item_gu(i + 2, e2, 0)
                item_down(i + 1, e1)
            item_gu(E - 1, E - 1, 1)
            item_down(E - 2, E - 2)

            more = sp.value_load(more_sb[0:1, 0:1], min_val=0, max_val=ROUNDS - 1)
            with sp.If(more > 0):
                with sp.Fori(0, more) as r:
                    with sp.Fori(0, E // 2) as pair:
                        e0 = sp.snap(2 * pair)
                        e1 = sp.snap(2 * pair + 1)
                        e_before = sp.snap((2 * pair + (E - 1)) % E)
                        before = sp.snap(r * E + 2 * pair + (E - 1))
                        item_down(before, e_before)
                        item_gu(before + 1, e0, 0)
                        item_down(before + 1, e0)
                        item_gu(before + 2, e1, 1)
            sp.wait_ge(gu_used, more * (8 * E) + 8 * (E - 1))
            for q in range(CH):
                sp.dma_start(down_last[:, 2 * q:2 * q + 2, :],
                             w_down[0, E - 1, 2 * q * P:(2 * q + 2) * P, :].rearrange("(k p) n -> p k n", p=P)
                             ).then_inc(last_landed[q], 16)
            sp.dma_start(g_fin_all, g_final.rearrange("(a n) -> a n", a=1).to_broadcast([P, D])
                         ).then_inc(gfin_landed, 16)
            for t in range(2):
                sp.wait_ge(fin, t + 1)
                sp.dma_start(y_prompt[0, t * P:(t + 1) * P, :], Y[:, t, :]).then_inc(stored, 16)
            sp.wait_ge(fin, 3)
            sp.dma_start(y_sample[:, 0, :], Y[0:SAMPLE, 2, :]).then_inc(stored, 16)
            sp.wait_ge(stored, 16 * 9)

        @block.gpsimd
        def _(pool):
            nc.gpsimd.memset(ident[:], 0.0).then_inc(consts, 1)
            nc.gpsimd.memset(below[:], 1.0).then_inc(consts, 1)
            nc.gpsimd.memset(table[:], -1.0).then_inc(consts, 1)
            nc.gpsimd.iota(scr_a.bitcast(I32)[:, 0:2 * SLOTS], pattern=[[0, 2], [1, SLOTS]], base=0,
                           channel_multiplier=0).then_inc(consts, 1)
            pool.wait_ge(consts, 4)
            nc.gpsimd.memset(table[:, :, NT:2 * NT], 0.0).then_inc(consts, 1)
            nc.gpsimd.affine_select(out=ident[:], in_=ident[:], compare_op=ALU.not_equal, fill=1.0, base=0,
                                    pattern=[[-1, P]], channel_multiplier=1).then_inc(consts, 1)
            nc.gpsimd.affine_select(out=below[:], in_=below[:], compare_op=ALU.is_gt, fill=0.0, base=0,
                                    pattern=[[1, P]], channel_multiplier=-1).then_inc(consts, 1)
            nc.gpsimd.tensor_copy(slot_no[:], scr_a.bitcast(I32)[:, 0:2 * SLOTS]).then_inc(consts, 1)

        @block.scalar
        def _(act):
            act.dma_start(Y[:, 0, :], x_prompt[0, 0:P, :]).then_inc(x_landed, 16)
            act.dma_start(Y[:, 1, :], x_prompt[0, P:2 * P, :]).then_inc(x_landed, 16)
            act.dma_start(Y[0:SAMPLE, 2, :], x_sample[:, 0, :]).then_inc(x_landed, 16)
            act.dma_start(Y[SAMPLE:SAMPLE + META, 2, :], meta_tokens).then_inc(x_landed, 16)
            def sum_squares(t, rows, squares):
                nc.scalar.activation(squares, Y[rows, t, :], ACT.Square,
                                     accum_out=stat[rows, 0, t:t + 1]).then_inc(squared, 1)

            act.wait_ge(x_landed, 64)
            act.wait_ge(dve, 2)
            for t in range(NT):
                rows = slice(0, P if t < 2 else SAMPLE + META)
                sum_squares(t, rows, XN1[rows, t, :])
            act.wait_ge(meaned, 1)
            nc.scalar.activation(stat[:, 2, :], stat[:, 1, :], ACT.Sqrt).then_inc(rooted, 1)

            act.dma_start(grp, w_pool_grp[0].rearrange("g c d -> c g d")).then_inc(grp_landed, 16)
            act.dma_start(new_pool_sample[0, :, 0:PBUF - 1, :], state_pool[0, :, 1:PBUF, :]).then_inc(stored, 16)
            act.dma_start(new_conv_sample[0, :, 0:CBUF - 1, :], state_conv[0, :, 1:CBUF, :]).then_inc(stored, 16)

            def round_block(b):
                act.wait_ge(win_landed[b % WIN_SLOTS], 16 * (b // WIN_SLOTS + 1))
                if b >= 2:
                    act.wait_ge(z_done, 2 * (b - 2) + 2)
                nc.scalar.activation(win_high[:, b % 2, :], gu_ring[:, b % WIN_SLOTS, :],
                                     ACT.Copy).then_inc(win_rounded, 1)

            def keep_z(n):
                if n < 12:
                    dst, cols = ((uT, COLS), (cT, COLS), (bT, TOK))[n // 4]
                    act.wait_ge(z_done, n + 1)
                    nc.scalar.activation(dst[:, n % 4, :], PS[:, n % 4, 0:cols], ACT.Copy).then_inc(z_kept, 1)
                elif n >= 16:
                    act.wait_ge(z_done, n + 1)
                    nc.scalar.activation(gatesT[:, n - 16, :], PS[:, n % 4, 0:TOK], ACT.Sigmoid).then_inc(z_kept, 1)

            round_block(0)
            for n, (high, whole) in enumerate(zip(h_pieces(h_high), h_pieces(hT))):
                act.wait_ge(h_scaled, n + 1)
                nc.scalar.activation(high, whole, ACT.Copy).then_inc(h_rounded, 1)
            round_block(1)
            for b in range(NCHUNK // 2):
                keep_z(2 * b)
                if b + 2 < NCHUNK // 2:
                    round_block(b + 2)
                keep_z(2 * b + 1)
                if b == 10:
                    act.wait_ge(tails_turned, 2)
                    nc.scalar.activation(tail_u[0:PBUF + SAMPLE, :], PS[0:PBUF + SAMPLE, 5, :],
                                         ACT.Copy).then_inc(tails_kept, 1)
                    nc.scalar.activation(tail_cv[0:CBUF + SAMPLE, :], PS[0:CBUF + SAMPLE, 6, :],
                                         ACT.Copy).then_inc(tails_kept, 1)
                    act.wait_ge(tails_kept, 2)
                    act.dma_start(new_pool_prompt[0, 0], tail_u[0:PBUF, :]).then_inc(stored, 16)
                    act.dma_start(new_pool_sample[0, :, PBUF - 1, :], tail_u[PBUF:PBUF + SAMPLE, :]
                                  ).then_inc(stored, 16)
                    act.dma_start(new_conv_prompt[0, 0], tail_cv[0:CBUF, :]).then_inc(stored, 16)
                    act.dma_start(new_conv_sample[0, :, CBUF - 1, :], tail_cv[CBUF:CBUF + SAMPLE, :]
                                  ).then_inc(stored, 16)
            act.wait_ge(z_done, 32)
            act.dma_start(g_ffn_all, g_ffn.to_broadcast([P, D])).then_inc(late_landed, 16)
            act.dma_start(bdown_rows, b_down[0]).then_inc(late_landed, 16)
            act.dma_start(wr[:], w_router[0].rearrange("(k p) e -> p k e", p=P)).then_inc(late_landed, 16)
            act.dma_start(br_all[:], b_router.to_broadcast([P, E])).then_inc(late_landed, 16)

            act.wait_ge(stored, 16 * 6)
            act.wait_ge(wo_done, 1)
            for q in range(4):
                nc.scalar.activation(samp_stage[:, 256 * q:256 * q + 256], PS[32 * q:32 * q + SAMPLE, 4, 0:256],
                                     ACT.Copy).then_inc(samp_staged, 1)

            def root(n, t, squares):
                rows = slice(0, P if t < 2 else SAMPLE)
                sum_squares(t, rows, squares)
                act.wait_ge(meaned, n + 1)
                nc.scalar.activation(stat[:, 2, t:t + 1], stat[:, 1, t:t + 1], ACT.Sqrt).then_inc(rooted, 1)

            def keep_parts(n, t):
                act.wait_ge(x2_turned, n + 1)
                rows = slice(0, P if t < 2 else SAMPLE)
                if t < 2:
                    for q in range(2):
                        nc.scalar.activation(xn2T[:, 4 * q:4 * q + 4, P * t:P * t + P],
                                             PS[:, (5 + 2 * t + q) % 8, :].rearrange("p (k t) -> p k t", k=4),
                                             ACT.Copy).then_inc(x2_kept, 1)
                else:
                    nc.scalar.activation(xn2T[:, :, 2 * P:TOK],
                                         PS[:, 1, 0:KT * SAMPLE].rearrange("p (k t) -> p k t", k=KT),
                                         ACT.Copy).then_inc(x2_kept, 1)
                dst = [XP[:, t, :], XP[:, 2 + t, :]] if t < 2 else \
                    [XP[at:at + SAMPLE, 6, :] for at in PARTS_AT[0:2]]
                nc.scalar.activation(dst[0], XN2[rows, t, :], ACT.Copy).then_inc(first_part, 1)
                act.wait_ge(first_rest, n + 1)
                nc.scalar.activation(dst[1], XN2[rows, t, :], ACT.Copy).then_inc(second_part, 1)

            for n, t in enumerate(ORDER):
                act.wait_ge(resid, n + 1)
                root(1 + n, t, XN2[0:P if t < 2 else SAMPLE, t, :])
                if t == 0:
                    keep_parts(0, ORDER[0])
                    keep_parts(1, ORDER[1])
            keep_parts(2, ORDER[2])
            act.wait_ge(shifted, 1)
            nc.scalar.activation(ex, ex, ACT.Exp).then_inc(exped, 1)
            act.wait_ge(gt_turned, 1)
            nc.scalar.activation(GT, PS[0:E, 4, 0:TOK], ACT.Copy).then_inc(gt_kept, 1)

            def keep_gathered(count):
                act.wait_ge(gathered, count)
                nc.scalar.activation(XgT[:].rearrange("p k s -> p (k s)"), PS[:, 5, :], ACT.Copy).then_inc(xg_ready, 1)

            keep_gathered(1)
            def back(i, way=spread):
                act.wait_ge(spread_turned, i + 1)
                nc.scalar.activation(way[:].rearrange("p t s -> p (t s)"), PS[:, 4, 0:NT * P],
                                     ACT.Copy).then_inc(spread_ready, 1)
                nc.scalar.activation(slot_gate[:], PS[:, 4, NT * P:NT * P + 1], ACT.Copy).then_inc(spread_ready, 1)

            def high(i):
                act.wait_ge(down_used, 4 * i + 4)
                act.wait_ge(spread_ready, 2 * i + 2)
                nc.scalar.activation(y_high[:], PS[:, 4, :], ACT.Copy, scale=slot_gate[:]).then_inc(high_ready, 1)

            def sigmoid(i):
                act.wait_ge(g_ready, i + 1)
                nc.scalar.activation(sig, hgu[:, 0:HALF], ACT.Sigmoid, scale=ALPHA).then_inc(sig_ready, 1)

            def item(i, first, before=0):
                if not first:
                    sigmoid(before)
                act.wait_ge(gu_used, 8 * i + 8)
                if not first:
                    act.wait_ge(act_ready, before + 1)
                nc.scalar.activation(hgu[:, 0:HALF], PS[:, 0, :], ACT.Copy).then_inc(gate_kept, 1)
                if not first:
                    back(before)
                keep_gathered(i + 2)
                if not first:
                    high(before)

            item(0, True)
            item(1, False)
            act.wait_ge(more_ready, 1)
            more = act.value_load(more_sb[0:1, 0:1], min_val=0, max_val=ROUNDS - 1)
            with act.Fori(0, more * E + (E - 2)) as m:
                item(m + 2, False, m + 1)
            last = more * E + (E - 1)
            sigmoid(last)
            back(last, spread_last)
            act.wait_ge(scattered, more * (3 * E) + 3 * (E - 1))
            high(last)
            for t in range(NT):
                act.wait_ge(added, more * (3 * E) + (3 * E + t + 1))
                root(4 + t, t, gu_ring[0:P if t < 2 else SAMPLE, 5 + t, 0:D])

        @block.tensor
        def _(pe):
            mm = nc.tensor.matmul
            pe.wait_ge(consts, 8)
            pe.wait_ge(rows_landed, 96)
            nc.tensor.transpose(PS[:, 4, 0:24], param_rows, ident[0:24, 0:24]).then_inc(rows_turned, 1)
            for c in range(16):
                last = nc.tensor.transpose(PS[:, 5, E * c:E * c + E], bgu_rows[:, P * c:P * c + P], ident[0:E, 0:E])
            last.then_inc(rows_turned, 1)
            n = SAMPLE * PBUF
            for c in range(CH):
                last = nc.tensor.transpose(PS[:, 6, n * c:n * c + n], pool_rows[:, P * c:P * c + P], ident[0:n, 0:n])
            last.then_inc(rows_turned, 1)
            n = SAMPLE * CBUF
            for c in range(CH):
                last = nc.tensor.transpose(PS[:, 7, n * c:n * c + n], conv_rows[:, P * c:P * c + P], ident[0:n, 0:n])
            last.then_inc(rows_turned, 1)

            pe.wait_ge(rows_kept, 1)
            for t in range(NT):
                pe.wait_ge(normed, 1 + t)
                rows = P if t < 2 else SAMPLE + META
                for k in range(KT):
                    out = PS[:, 2 * t + k // 4, P * (k % 4):P * (k % 4) + P] if t < 2 else PS[:, 4, rows * k:rows * k + rows]
                    last = nc.tensor.transpose(out, XN1[0:rows, t, P * k:P * k + P], ident[0:rows, 0:rows])
                last.then_inc(x_turned, 1)

            pe.wait_ge(h_ready, 6)
            for n in range(NCHUNK):
                lo = 0 if n < 8 or 12 <= n < 16 else META
                b = n // 2
                pe.wait_ge(win_ready, b + 1)
                if n >= 4:
                    z_evacuated(pe, n - 4)
                w_high, w_low = (part.rearrange("p (k n) -> p k n", k=KT)
                                 for part in (win_high[:, b % 2, :], win_low[:, b % WIN_SLOTS, :]))
                for k in range(KT):
                    for part, (w, h) in enumerate(((w_high, h_high), (w_high, h_low), (w_low, h_high))):
                        last = mm(PS[:, n % 4, 0:COLS - lo], w[:, k, P * (n % 2):P * (n % 2) + P], h[:, k, lo:COLS],
                                  start=(k == 0 and part == 0), stop=(k == KT - 1 and part == 2))
                last.then_inc(z_done, 1)
                if n == 19:
                    pe.wait_ge(cv_done, 4)
                    pe.wait_ge(rows_kept, 5)
                    for c in range(CH):
                        last = nc.tensor.transpose(PS[0:PBUF + SAMPLE, 5, P * c:P * c + P],
                                                   uT[:, c, COLS - SAMPLE - PBUF:COLS], ident[:])
                    last.then_inc(tails_turned, 1)
                    for c in range(CH):
                        last = nc.tensor.transpose(PS[0:CBUF + SAMPLE, 6, P * c:P * c + P],
                                                   cvT[:, c, COLS - SAMPLE - CBUF:COLS], ident[:])
                    last.then_inc(tails_turned, 1)
                if n == 23:
                    pe.wait_ge(tails_kept, 2)
                    pe.wait_ge(pm_ready, 4)
                    pe.wait_ge(grp_landed, 16)
                    for g in range(CH):
                        mm(PS[:, 4 + g, 0:TOK], grp[:, g, :], pmT[:, g, :], start=True, stop=True
                           ).then_inc(grp_done, 1)

            pe.wait_ge(pa_ready, 4)
            pe.wait_ge(cb_ready, 4)
            pe.wait_ge(up_landed, 16)
            pe.wait_ge(convout_landed, 16)
            for m in range(KT):
                if m >= 2:
                    pe.wait_ge(mixed, m - 1)
                for k in range(CH):
                    mm(PS[:, 4 + 2 * (m % 2), 0:TOK], pool_up[:, k, P * m:P * m + P], paT[:, k, :],
                       start=(k == 0), stop=(k == CH - 1))
                for k in range(CH):
                    last = mm(PS[:, 5 + 2 * (m % 2), 0:TOK], conv_out[:, k, P * m:P * m + P], cbT[:, k, :],
                              start=(k == 0), stop=(k == CH - 1))
                last.then_inc(branches, 1)

            pe.wait_ge(mixed, 8)
            pe.wait_ge(wo_landed, 16)
            pe.wait_ge(z_kept, 28)
            for k in range(KT):
                for q in range(4):
                    last = mm(PS[32 * q:32 * q + SAMPLE, 4, 0:256], mT_samp[:, k, :],
                              down_ring[:, k, 256 * q:256 * q + 256], start=(k == 0), stop=(k == KT - 1))
            last.then_inc(wo_done, 1)

            def out_project(t, h):
                for k in range(KT):
                    last = mm(PS[:, 2 * t + h, :], mT[:, k, P * t:P * t + P],
                              down_ring[:, k, HALF * h:HALF * h + HALF], start=(k == 0), stop=(k == KT - 1))
                last.then_inc(wo_done, 1)

            def turn_rows(n, t):
                pe.wait_ge(normed, 4 + n)
                rows = P if t < 2 else SAMPLE
                for k in range(KT):
                    bank = (5 + 2 * t + k // 4) % 8
                    out = PS[:, bank, P * (k % 4):P * (k % 4) + P] if t < 2 else PS[:, 1, rows * k:rows * k + rows]
                    last = nc.tensor.transpose(out, XN2[0:rows, t, P * k:P * k + P], ident[0:rows, 0:rows])
                last.then_inc(x2_turned, 1)

            def route_rows(n, t):
                pe.wait_ge(x2_kept, (1, 3, 5)[n])
                rows = P if t < 2 else SAMPLE
                for k in range(KT):
                    last = mm(PS[0:rows, 4, E * t:E * t + E], xn2T[:, k, P * t:P * t + rows], wr[:, k, :],
                              start=(k == 0), stop=(k == KT - 1))
                last.then_inc(logits_done, 1)

            out_project(0, 0)
            out_project(0, 1)
            out_project(1, 0)
            pe.wait_ge(resid, 2)
            turn_rows(0, 2)
            turn_rows(1, 0)
            out_project(1, 1)
            pe.wait_ge(late_landed, 64)
            route_rows(0, 2)
            route_rows(1, 0)
            turn_rows(2, 1)
            route_rows(2, 1)

            pe.wait_ge(mask_ready, 1)
            for t in range(NT):
                for s in range(t + 1):
                    mm(PS[:, 3, E * t:E * t + E], below_small[:] if s == t else ones[:], mask_small[:, s, :],
                       start=(s == 0), stop=(s == t))
            for s in range(NT):
                last = mm(PS[:, 3, E * NT:E * NT + E], ones[:], mask_small[:, s, :], start=(s == 0), stop=(s == NT - 1))
            last.then_inc(ranks, 1)
            pe.wait_ge(mask_ready, 2)
            for t in range(NT):
                rows = P if t < 2 else SAMPLE
                last = nc.tensor.transpose(PS[0:E, 4, P * t:P * t + rows], G[0:rows, t, :], ident[0:rows, 0:rows])
            last.then_inc(gt_turned, 1)

            def gather():
                parts = ((0, 0), (2, 0), (4, 0), (1, 1), (3, 1), (5, 1), (6, 2))
                for k in range(KT):
                    for n, (part, t) in enumerate(parts):
                        last = mm(PS[:, 5, SLOTS * k:SLOTS * k + SLOTS], XP[:, part, P * k:P * k + P], pick[:, t, :],
                                  start=(n == 0), stop=(n == len(parts) - 1))
                last.then_inc(gathered, 1)

            def scatter(t, way=spread, bank=6):
                for h in range(2):
                    rows = slice(SLOTS * h, SLOTS * h + SLOTS)
                    mm(PS[:, bank + h, :], way[rows, t, :], y_high[rows, :], start=True, stop=False)
                    last = mm(PS[:, bank + h, :], way[rows, t, :], y_low[rows, :], start=False, stop=True)
                last.then_inc(scattered, 1)

            pe.wait_ge(third_part, NT)
            pe.wait_ge(pick_ready, 1)
            gather()

            def down_bias():
                pe.wait_ge(gt_kept, 1)
                for t in range(NT):
                    rows = P if t < 2 else SAMPLE
                    if t:
                        pe.wait_ge(added, t)
                    for h in range(2):
                        last = mm(PS[0:rows, 6 + h, :], GT[:, P * t:P * t + rows],
                                  bdown_rows[:, HALF * h:HALF * h + HALF], start=True, stop=True)
                    last.then_inc(bd_done, 1)

            def scatter_item(i, t):
                if t == 0:
                    pe.wait_ge(low_ready, i + 1)
                pe.wait_ge(added, 3 * i + (t + 3))
                scatter(t)

            def gate_up(i, u, landed, two_before):
                pe.wait_ge(xg_ready, i + 1)
                for k in range(KT):
                    pe.wait_ge(gu_landed[KT * u + k], landed)
                    w = gu_ring[:, KT * u + k, :]
                    for b in range(2):
                        for h in range(2):
                            last = mm(PS[SLOTS * h:SLOTS * h + SLOTS, b, :], XgT[:, k, :],
                                      w[:, D * b + HALF * h:D * b + HALF * h + HALF],
                                      start=(k == 0), stop=(k == KT - 1))
                    last.then_inc(gu_used, 1)
                    if two_before is not None and k in (2, 4, 6):
                        scatter_item(two_before, k // 2 - 1)

            def way_back(i):
                pe.wait_ge(twice_ready, i + 1)
                for t in range(NT):
                    nc.tensor.transpose(PS[:, 4, P * t:P * t + P], pick_twice[:, t, :], ident[:])
                for t in range(NT):
                    last = mm(PS[:, 4, NT * P:NT * P + 1], pick_twice[:, t, :], cur_back[:, NT + t:NT + t + 1],
                              start=(t == 0), stop=(t == NT - 1))
                last.then_inc(spread_turned, 1)

            def down(i, weights=down_ring, landed=None, before=None):
                pe.wait_ge(spread_ready, 2 * i + 2)
                pe.wait_ge(act_ready, i + 1)
                for f in range(KT):
                    if f % 2 == 0:
                        if landed:
                            pe.wait_ge(landed[f // 2], 16)
                        else:
                            pe.wait_ge(down_landed[f // 2], 16 * i + 16)
                    for h in range(2):
                        last = mm(PS[SLOTS * h:SLOTS * h + SLOTS, 4, :], actT[:, f % 4, f // 4, :],
                                  weights[:, f, HALF * h:HALF * h + HALF], start=(f == 0), stop=(f == KT - 1))
                    if f % 2:
                        last.then_inc(down_used, 1)
                    if before is not None and f in (1, 3):
                        scatter_item(before, f // 2 + 1)

            def turn(i):
                pe.wait_ge(gate_kept, i + 1)
                for j in range(CH):
                    last = nc.tensor.transpose(PS[:, 2, P * j:P * j + P], hgu[:, P * j:P * j + P], ident[:])
                last.then_inc(gate_turned, 1)
                pe.wait_ge(up_kept, i + 1)
                for j in range(CH):
                    last = nc.tensor.transpose(PS[:, 3, P * j:P * j + P], hgu[:, HALF + P * j:HALF + P * j + P],
                                               ident[:])
                last.then_inc(up_turned, 1)

            def item(i, u, landed, before=None, two_before=None, bias=False):
                gate_up(i, u, landed, two_before)
                if bias:
                    down_bias()
                if before is not None:
                    way_back(before)
                pe.wait_ge(pick_ready, i + 2)
                gather()
                if before is not None:
                    down(before)
                turn(i)

            item(0, 0, 16)
            item(1, 1, 16, 0, bias=True)
            pe.wait_ge(more_ready, 1)
            more = pe.value_load(more_sb[0:1, 0:1], min_val=0, max_val=ROUNDS - 1)
            with pe.Fori(0, more * (E // 2) + (E // 2 - 1)) as pair:
                item(2 * pair + 2, 0, 16 * pair + 32, 2 * pair + 1, 2 * pair)
                item(2 * pair + 3, 1, 16 * pair + 32, 2 * pair + 2, 2 * pair + 1)
            last, before = more * E + (E - 1), more * E + (E - 2)
            pe.wait_ge(low_ready, before + 1)
            way_back(last)
            scatter_item(before, 0)
            down(last, down_last, last_landed, before)
            pe.wait_ge(low_ready, last + 1)
            pe.wait_ge(added, more * (3 * E) + 3 * E)
            for t in range(NT):
                scatter(t, spread_last, LAST_BANKS[t])

        @block.vector
        def _(v):
            tt, ts, stt = nc.vector.tensor_tensor, nc.vector.tensor_scalar, nc.vector.scalar_tensor_tensor
            count = [0]

            def step(ins):
                count[0] += 1
                ins.then_inc(dve, 1)
                v.wait_ge(dve, count[0])

            def mark(ins):
                count[0] += 1
                ins.then_inc(dve, 1)

            def done():
                v.wait_ge(dve, count[0])

            mark(nc.vector.memset(stat[:], 1.0))
            mark(nc.vector.memset(XP[:, 6, :], 0.0))
            v.wait_ge(rows_turned, 4)
            nc.vector.tensor_copy(params[:], PS[:, 4, 0:24]).then_inc(rows_kept, 1)
            for b in range(2):
                nc.vector.tensor_copy(bias_gu[:, :, b, :, :].rearrange("p e j h -> p h j e"),
                                      PS[:, 5, 256 * b:256 * b + 256].rearrange("p (h j e) -> p h j e", h=2, j=CH)
                                      ).then_inc(rows_kept, 1)
            v.wait_ge(consts, 8)
            nc.vector.tensor_copy(poolT, PS[:, 6, 0:480].rearrange("p (c b r) -> p c b r", c=CH, r=PBUF)
                                  ).then_inc(rows_kept, 1)
            nc.vector.tensor_copy(convT, PS[:, 7, 0:64].rearrange("p (c b r) -> p c b r", c=CH, r=CBUF)
                                  ).then_inc(rows_kept, 1)

            def rstd(n, tiles):
                ts(stat[:, 1, tiles], stat[:, 0, tiles], 1.0 / D, EPS, ALU.mult, ALU.add).then_inc(meaned, 1)
                v.wait_ge(rooted, n + 1)
                step(nc.vector.reciprocal(stat[:, 3, tiles], stat[:, 2, tiles]))

            v.wait_ge(squared, NT)
            done()
            rstd(0, slice(0, NT))
            for t in range(NT):
                rows = slice(0, P if t < 2 else SAMPLE + META)
                ts(XN1[rows, t, :], Y[rows, t, :], stat[rows, 3, t:t + 1], None, ALU.mult).then_inc(normed, 1)
            def low_block(b):
                v.wait_ge(win_rounded, b + 1)
                tt(win_low[:, b % WIN_SLOTS, :], gu_ring[:, b % WIN_SLOTS, :],
                   win_high[:, b % 2, :].bitcast(F32), ALU.subtract).then_inc(win_ready, 1)

            low_block(0)
            v.wait_ge(rows_kept, 1)
            pieces = h_pieces(hT)
            for t in range(NT):
                v.wait_ge(x_turned, t + 1)
                if t < 2:
                    for q in range(2):
                        tt(pieces[2 * t + q], PS[:, 2 * t + q, :].rearrange("p (k t) -> p k t", k=4),
                           params[:, 4 * q:4 * q + 4].unsqueeze(2).to_broadcast([P, 4, P]), ALU.mult
                           ).then_inc(h_scaled, 1)
                else:
                    src = PS[:, 4, 0:KT * (SAMPLE + META)].rearrange("p (k t) -> p k t", k=KT)
                    tt(pieces[4], src[:, :, 0:SAMPLE],
                       params[:, 0:8].unsqueeze(2).to_broadcast([P, KT, SAMPLE]), ALU.mult).then_inc(h_scaled, 1)
                    tt(pieces[5], src[:, :, SAMPLE:SAMPLE + META],
                       params[:, 0:8].unsqueeze(2).to_broadcast([P, KT, META]), ALU.mult).then_inc(h_scaled, 1)
            for n, (whole, high, rest) in enumerate(zip(pieces, h_pieces(h_high), h_pieces(h_low))):
                v.wait_ge(h_scaled, n + 1)
                v.wait_ge(h_rounded, n + 1)
                tt(rest, whole, high.bitcast(F32), ALU.subtract).then_inc(h_ready, 1)
            low_block(1)

            end = META + PROMPT

            def pooling(g, w):
                src, span, bufs = uT[:, g, :], 1, [scr_a, scr_b]
                while span < w:
                    dst = bufs[0]
                    lo = 2 * span - 1
                    step(tt(dst[:, lo:end], src[:, lo:end], src[:, lo - span:end - span], ALU.add))
                    src, span, bufs = dst, 2 * span, bufs[::-1]
                step(stt(pmT[:, g, 0:PROMPT], src[:, META:end], 1.0 / w, uT[:, g, META:end], ALU.mult,
                         ALU.subtract))
                step(nc.vector.tensor_reduce(scr_a[:, 0:SAMPLE], poolT[:, g, :, PBUF + 1 - w:PBUF], AXX, ALU.add))
                step(tt(scr_a[:, 0:SAMPLE], scr_a[:, 0:SAMPLE], uT[:, g, end:COLS], ALU.add))
                stt(pmT[:, g, PROMPT:TOK], scr_a[:, 0:SAMPLE], 1.0 / w, uT[:, g, end:COLS], ALU.mult,
                    ALU.subtract).then_inc(pm_ready, 1)
                v.wait_ge(pm_ready, g + 1)

            def gated_value(c):
                v.wait_ge(z_done, 13 + c)
                tt(cvT[:, c, :], PS[:, c, 0:COLS], cT[:, c, :], ALU.mult).then_inc(cv_done, 1)

            def convolution(c):
                v.wait_ge(cv_done, c + 1)
                tap = [params[:, 12 + 4 * k + c:13 + 4 * k + c] for k in range(CW)]
                acc, accs = scr_a[:, 0:PROMPT], scr_a[:, PROMPT:TOK]
                cv = cvT[:, c, :]
                mark(ts(acc, cv[:, META - 2:end - 2], tap[0], None, ALU.mult))
                step(ts(accs, convT[:, c, :, 0], tap[0], None, ALU.mult))
                mark(stt(acc, cv[:, META - 1:end - 1], tap[1], acc, ALU.mult, ALU.add))
                step(stt(accs, convT[:, c, :, 1], tap[1], accs, ALU.mult, ALU.add))
                mark(stt(acc, cv[:, META:end], tap[2], acc, ALU.mult, ALU.add))
                step(stt(accs, cv[:, end:COLS], tap[2], accs, ALU.mult, ALU.add))
                tt(cbT[:, c, :], scr_a[:, 0:TOK], bT[:, c, :], ALU.mult).then_inc(cb_ready, 1)
                v.wait_ge(cb_ready, c + 1)

            for b in range(NCHUNK // 2):
                if b + 2 < NCHUNK // 2:
                    low_block(b + 2)
                if b == 2:
                    v.wait_ge(z_kept, 4)
                    v.wait_ge(rows_kept, 5)
                if 2 <= b < 6:
                    pooling(b - 2, WINDOWS[b - 2])
                if b in (6, 7):
                    v.wait_ge(z_kept, 12)
                    gated_value(2 * (b - 6))
                    gated_value(2 * (b - 6) + 1)
                if 8 <= b < 12:
                    convolution(b - 8)
                if b == 12:
                    for g in range(CH):
                        v.wait_ge(grp_done, g + 1)
                        ts(paT[:, g, :], PS[:, 4 + g, 0:TOK], params[:, 8 + g:9 + g], None, ALU.mult
                           ).then_inc(pa_ready, 1)

            v.wait_ge(z_kept, 28)
            for m in range(KT):
                v.wait_ge(branches, m + 1)
                mark(tt(scr_b[:, 0:TOK], PS[:, 4 + 2 * (m % 2), 0:TOK], gatesT[:, m, :], ALU.mult))
                step(tt(scr_a[:, 0:TOK], PS[:, 5 + 2 * (m % 2), 0:TOK], gatesT[:, KT + m, :], ALU.mult))
                mark(tt(mT[:, m, :], scr_b[:, 0:PROMPT], scr_a[:, 0:PROMPT], ALU.add))
                done()
                tt(mT_samp[:, m, :], scr_b[:, PROMPT:TOK], scr_a[:, PROMPT:TOK], ALU.add).then_inc(mixed, 1)
                v.wait_ge(mixed, m + 1)

            mark(nc.vector.memset(ones[:], 1.0))
            mark(nc.vector.tensor_copy(below_small[:], below[:]))
            mark(nc.vector.memset(logits, 0.0))
            mark(nc.vector.memset(valid[:, 0:2], 1.0))
            mark(nc.vector.memset(valid[:, 2:3], 0.0))
            for r in range(1, ROUNDS):
                mark(nc.vector.memset(bounds[:, r - 1:r], float(SLOTS * r)))
            done()
            step(nc.vector.memset(valid[0:SAMPLE, 2:3], 1.0))

            def residual(n, t):
                rows = slice(0, P if t < 2 else SAMPLE)
                if t < 2:
                    v.wait_ge(wo_done, 2 * t + 3)
                    tt(Y[:, t, :].rearrange("p (h n) -> p h n", h=2), PS[:, 2 * t:2 * t + 2, :],
                       Y[:, t, :].rearrange("p (h n) -> p h n", h=2), ALU.add).then_inc(resid, 1)
                else:
                    v.wait_ge(samp_staged, 4)
                    tt(Y[rows, 2, :], samp_stage, Y[rows, 2, :], ALU.add).then_inc(resid, 1)
                v.wait_ge(squared, NT + n + 1)
                rstd(1 + n, slice(t, t + 1))
                stt(XN2[rows, t, :], Y[rows, t, :], stat[rows, 3, t:t + 1], g_ffn_all[rows, :], ALU.mult,
                    ALU.mult).then_inc(normed, 1)

            def rest_parts(n, t):
                rows = slice(0, P if t < 2 else SAMPLE)
                src = [XP[:, t, :], XP[:, 2 + t, :], XP[:, 4 + t, :]] if t < 2 else \
                    [XP[at:at + SAMPLE, 6, :] for at in PARTS_AT]
                v.wait_ge(first_part, n + 1)
                if t < 2:
                    tt(XN2[rows, t, :], XN2[rows, t, :], src[0], ALU.subtract).then_inc(first_rest, 1)
                    v.wait_ge(second_part, n + 1)
                    tt(src[2], XN2[rows, t, :], src[1], ALU.subtract).then_inc(third_part, 1)
                else:
                    tt(XN2[rows, t, :], XN2[rows, t, :], src[0], ALU.subtract).then_inc(first_rest, 1)
                    v.wait_ge(second_part, n + 1)
                    step(nc.vector.tensor_copy(samp_second[:], src[1]))
                    tt(src[2], XN2[rows, t, :], samp_second[:], ALU.subtract).then_inc(third_part, 1)

            v.wait_ge(late_landed, 64)
            residual(0, 2)
            residual(1, 0)
            rest_parts(0, 2)
            rest_parts(1, 0)
            residual(2, 1)
            rest_parts(2, 1)

            v.wait_ge(logits_done, NT)
            for t in range(NT):
                rows = slice(0, P if t < 2 else SAMPLE)
                mark(tt(logits[rows, t, :], PS[rows, 4, E * t:E * t + E], br_all[rows, :], ALU.add))
            done()
            for t in range(NT):
                mark(nc.vector.max(top[:, t, :], logits[:, t, :]))
            done()
            tt(ex, top[:, :, 0:TOPK], top[:, :, 0:1].to_broadcast([P, NT, TOPK]), ALU.subtract).then_inc(shifted, 1)
            for t in range(NT):
                mark(nc.vector.max_index(topi[:, t, :].bitcast(U32), top[:, t, :], logits[:, t, :]))
            done()
            step(nc.vector.tensor_copy(topf, topi.bitcast(U32)))
            for t in range(NT):
                mark(tt(hot[:, t, :, :], slot_no[:, 0:E].unsqueeze(1).to_broadcast([P, TOPK, E]),
                        topf[:, t, 0:TOPK].unsqueeze(2).to_broadcast([P, TOPK, E]), ALU.is_equal))
            done()
            step(nc.vector.tensor_reduce(mask, hot.rearrange("p t k e -> p t e k"), AXX, ALU.add))
            tt(mask_small[:], mask, valid.unsqueeze(2).to_broadcast([P, NT, E]), ALU.mult).then_inc(mask_ready, 1)
            v.wait_ge(exped, 1)
            step(nc.vector.tensor_reduce(exs, ex, AXX, ALU.add))
            step(nc.vector.reciprocal(exs, exs))
            step(tt(ex, ex, exs.unsqueeze(2).to_broadcast([P, NT, TOPK]), ALU.mult))
            for t in range(NT):
                mark(tt(hotg[:, t, :, :], hot[:, t, :, :], ex[:, t, :].unsqueeze(2).to_broadcast([P, TOPK, E]),
                        ALU.mult))
            done()
            nc.vector.tensor_reduce(G, hotg.rearrange("p t k e -> p t e k"), AXX, ALU.add).then_inc(mask_ready, 1)
            v.wait_ge(mask_ready, 2)
            v.wait_ge(ranks, 1)
            step(stt(pos1, PS[:, 3, 0:NT * E].rearrange("p (t e) -> p t e", e=E), 1.0, mask_small[:],
                     ALU.add, ALU.mult))

            def fill_slots(r):
                step(ts(table[:, E * r:E * r + E, 0:NT].rearrange("p e t -> p t e"), pos1, -1.0 - SLOTS * r, None,
                        ALU.add))
                for at in PARTS_AT[1:]:
                    mark(nc.vector.tensor_copy(table[at:at + SAMPLE, E * r:E * r + E, NT - 1],
                                               table[0:SAMPLE, E * r:E * r + E, NT - 1]))
                done()

            def make_pick(i):
                nc.vector.tensor_copy(cur[:], table[:, i, 0:NT] if type(i) is int else
                                      table[:, bass.ds(i, 1), 0:NT].rearrange("p a t -> p (a t)")
                                      ).then_inc(cur_ready, 1)
                v.wait_ge(cur_ready, i + 1)
                if type(i) is not int or i > 0:
                    v.wait_ge(gathered, i)
                tt(pick[:], slot_no[:, 0:SLOTS].unsqueeze(1).to_broadcast([P, NT, SLOTS]),
                   cur[:].unsqueeze(2).to_broadcast([P, NT, SLOTS]), ALU.is_equal).then_inc(pick_ready, 1)

            def make_twice(i):
                nc.vector.tensor_copy(cur_back[:], table[:, i, :] if type(i) is int else
                                      table[:, bass.ds(i, 1), :].rearrange("p a t -> p (a t)")
                                      ).then_inc(back_ready, 1)
                v.wait_ge(back_ready, i + 1)
                tt(pick_twice[:], slot_no[:].unsqueeze(1).to_broadcast([P, NT, 2 * SLOTS]),
                   cur_back[:, 0:NT].unsqueeze(2).to_broadcast([P, NT, 2 * SLOTS]), ALU.is_equal
                   ).then_inc(twice_ready, 1)

            fill_slots(0)
            make_pick(0)
            for r in range(ROUNDS):
                if r:
                    fill_slots(r)
                for t in range(NT):
                    rows = slice(0, P if t < 2 else SAMPLE)
                    mark(nc.vector.tensor_copy(table[rows, E * r:E * r + E, NT + t], G[rows, t, :]))
            done()
            step(nc.vector.tensor_reduce(most, PS[:, 3, NT * E:NT * E + E], AXX, ALU.max))
            step(tt(over, bounds, most.to_broadcast([P, ROUNDS - 1]), ALU.is_lt))
            step(nc.vector.tensor_reduce(most, over, AXX, ALU.add))
            nc.vector.tensor_copy(more_sb[:], most).then_inc(more_ready, 1)
            v.wait_ge(gt_kept, 1)
            v.wait_ge(more_ready, 1)
            more = v.value_load(more_sb[0:1, 0:1], min_val=0, max_val=ROUNDS - 1)
            nc.vector.memset(done_mark[:], 0.0).then_inc(more_ready, 1)

            def add_rows(i, t, bank=6):
                rows = slice(0, P if t < 2 else SAMPLE)
                v.wait_ge(scattered, 3 * i + (t + 1))
                tt(Y[rows, t, :].rearrange("p (h n) -> p h n", h=2), PS[rows, bank:bank + 2, :],
                   Y[rows, t, :].rearrange("p (h n) -> p h n", h=2), ALU.add).then_inc(added, 1)

            gate, up = hgu[:, 0:HALF], hgu[:, HALF:2 * HALF]

            def biased(b, e):
                bias = bias_gu[:, e, b, :, :].rearrange("p j h -> p (j h)") if type(e) is int else \
                    bias_gu[:, bass.ds(e, 1), b, :, :].rearrange("p a j h -> p (a j h)")
                tt(hgu[:, HALF * b:HALF * b + HALF].rearrange("p (c s) -> p c s", s=SLOTS),
                   PS[:, 2 + b, :].rearrange("p (c s) -> p c s", s=SLOTS),
                   bias.unsqueeze(2).to_broadcast([P, 8, SLOTS]), ALU.add).then_inc((g_biased, u_biased)[b], 1)

            def swiglu(i, e):
                v.wait_ge(gate_turned, i + 1)
                v.wait_ge(up_turned, i + 1)
                biased(0, e)
                v.wait_ge(g_biased, i + 1)
                ts(gate, gate, LIMIT, None, ALU.min).then_inc(g_ready, 1)
                biased(1, e)
                v.wait_ge(u_biased, i + 1)
                ts(up, up, LIMIT, -LIMIT, ALU.min, ALU.max).then_inc(u_ready, 1)
                v.wait_ge(u_ready, i + 1)
                v.wait_ge(g_ready, i + 1)
                stt(up, up, 1.0, gate, ALU.add, ALU.mult).then_inc(gu_product, 1)
                v.wait_ge(gu_product, i + 1)
                v.wait_ge(sig_ready, i + 1)
                tt(actT[:].rearrange("p j h s -> p (j h s)"), up, sig, ALU.mult).then_inc(act_ready, 1)

            def low_part(i):
                v.wait_ge(high_ready, i + 1)
                stt(y_low[:], PS[:, 4, :], slot_gate[:], y_high[:].bitcast(F32), ALU.mult,
                    ALU.subtract).then_inc(low_ready, 1)

            def add_bias(t):
                rows = slice(0, P if t < 2 else SAMPLE)
                v.wait_ge(bd_done, t + 1)
                tt(Y[rows, t, :].rearrange("p (h n) -> p h n", h=2), PS[rows, 6:8, :],
                   Y[rows, t, :].rearrange("p (h n) -> p h n", h=2), ALU.add).then_inc(added, 1)

            def item(i, after, before=None, e_before=0, two_before=None):
                if before is not None:
                    swiglu(before, e_before)
                if two_before is not None:
                    for t in range(NT):
                        add_rows(two_before, t)
                if before is not None:
                    make_twice(before)
                make_pick(after)
                v.wait_ge(gu_used, 8 * i + 8)
                if before is not None:
                    v.wait_ge(act_ready, before + 1)
                nc.vector.tensor_copy(up, PS[:, 1, :]).then_inc(up_kept, 1)
                if type(i) is int and i == 1:
                    for t in range(NT):
                        add_bias(t)
                if before is not None:
                    low_part(before)

            item(0, 1)
            item(1, 2, 0)
            with v.Fori(0, more * E + (E - 2)) as m:
                item(m + 2, m + 3, m + 1, (m + 1) % E, m)
            last, before = more * E + (E - 1), more * E + (E - 2)
            make_twice(last)
            swiglu(last, E - 1)
            for t in range(NT):
                add_rows(before, t)
            low_part(last)
            for t in range(NT):
                add_rows(last, t, LAST_BANKS[t])
            v.wait_ge(gfin_landed, 16)
            for t in range(NT):
                rows = slice(0, P if t < 2 else SAMPLE)
                v.wait_ge(squared, 2 * NT + t + 1)
                rstd(4 + t, slice(t, t + 1))
                stt(Y[rows, t, :], Y[rows, t, :], stat[rows, 3, t:t + 1], g_fin_all[rows, :], ALU.mult,
                    ALU.mult).then_inc(fin, 1)


_INS = ['x_prompt', 'x_sample', 'state_pool', 'state_conv', 'meta_tokens', 'g_mix', 'w_in', 'w_pool_grp', 'pool_scale',
        'w_pool_up', 'w_conv', 'w_conv_out', 'w_o', 'g_ffn', 'w_router', 'b_router', 'w_gu', 'b_gu', 'w_down', 'b_down',
        'g_final']
_OUTS = [((1, PROMPT, D), 'float32'), ((SAMPLE, 1, D), 'float32'), ((1, 1, PBUF, HALF), 'float32'),
         ((1, 1, CBUF, HALF), 'float32'), ((1, SAMPLE, PBUF, HALF), 'float32'), ((1, SAMPLE, CBUF, HALF), 'float32')]


def kernel(**inputs):
    import numpy as _np
    import concourse.bacc as _bacc
    from concourse import mybir as _mybir
    from concourse.bass_utils import run_bass_kernel_spmd as _run

    nc = _bacc.Bacc("TRN2", target_bir_lowering=False, num_devices=1, dynamic_dma_scratch_size=1024)
    arrays, args = {}, []
    for name in _INS:
        a = _np.ascontiguousarray(inputs[name])
        arrays[f"in_{name}_dram"] = a
        args.append(nc.dram_tensor(f"in_{name}_dram", a.shape, _mybir.dt.from_np(a.dtype), kind="ExternalInput").ap())
    for i, (shape, dtype) in enumerate(_OUTS):
        dt = _mybir.dt.from_np(_np.dtype(dtype))
        args.append(nc.dram_tensor(f"out_{i}_dram", shape, dt, kind="ExternalOutput").ap())
    build(nc, *args)
    r = _run(nc, [arrays], core_ids=[0])
    return tuple(r.results[0][f"out_{i}_dram"] for i in range(len(_OUTS)))
```
